# Optimizing a Trainium2 kernel written in Bass

```python
import math
import jax, jax.numpy as jnp
from jax import lax
import numpy as np

D_MODEL = 1024
BATCH = 1
SEQ = 256
DEPTH = 2

D_MIX = D_MODEL
ATTN_WIDTH = D_MIX // 2
N_SB_HEADS = 8
SB_HEAD_DIM = ATTN_WIDTH // N_SB_HEADS
POOL_WINDOWS = (2, 4, 8, 16)
N_POOL_GROUPS = len(POOL_WINDOWS)
POOL_WIDTH = D_MIX // 4
POOL_GROUP_DIM = POOL_WIDTH // N_POOL_GROUPS
CONV_WIDTH = D_MIX - ATTN_WIDTH - POOL_WIDTH
CONV_KERNEL = 31
IN_COLS = 3 * ATTN_WIDTH + POOL_WIDTH + 2 * CONV_WIDTH
Q_BLOCK = 128

D_FF = 2816
N_EXPERTS = 8
TOP_K = 2
N_DENSE = (DEPTH + 1) // 2
N_MOE = DEPTH // 2

RMS_EPS = 1e-6
LN_EPS = 1e-5

kernel_name = "hybrid_sbattn_pool_conformer_moe"

def rmsnorm(x, g):
    x32 = x.astype(jnp.float32)
    y = x32 * lax.rsqrt(jnp.mean(x32 * x32, axis=-1, keepdims=True) + RMS_EPS)
    return (y * g.astype(jnp.float32)).astype(x.dtype)

def layernorm(x, g, b):
    x32 = x.astype(jnp.float32)
    mu = jnp.mean(x32, axis=-1, keepdims=True)
    xc = x32 - mu
    var = jnp.mean(xc * xc, axis=-1, keepdims=True)
    y = xc * lax.rsqrt(var + LN_EPS)
    return (y * g.astype(jnp.float32) + b.astype(jnp.float32)).astype(x.dtype)

def _sb_block(qb, k_pre, v_pre, q_start):
    scale = 1.0 / math.sqrt(SB_HEAD_DIM)
    z = jnp.einsum('bqhd,bkhd->bhqk', qb, k_pre).astype(jnp.float32) * scale
    t_idx = q_start + jnp.arange(qb.shape[1])
    s_idx = jnp.arange(k_pre.shape[1])
    mask = s_idx[None, :] < t_idx[:, None]
    log_1m_beta = jnp.where(mask, jax.nn.log_sigmoid(-z), 0.0)
    rest = lax.cumsum(log_1m_beta, axis=3, reverse=True) - log_1m_beta
    w = jnp.where(mask, jnp.exp(jax.nn.log_sigmoid(z) + rest), 0.0)
    return jnp.einsum('bhqk,bkhd->bqhd', w.astype(v_pre.dtype), v_pre)

def stick_breaking_attention(q, k, v):
    S = q.shape[1]
    outs = []
    for start in range(0, S, Q_BLOCK):
        end = start + Q_BLOCK
        outs.append(_sb_block(q[:, start:end], k[:, :end], v[:, :end], start))
    return jnp.concatenate(outs, axis=1)

def multiscale_pool(u, w_pool, pool_scale):
    B, S, _ = u.shape
    ug = u.reshape(B, S, N_POOL_GROUPS, POOL_GROUP_DIM).astype(jnp.float32)
    csum = jnp.cumsum(ug, axis=1)
    pos = jnp.arange(S)
    outs = []
    for g, win in enumerate(POOL_WINDOWS):
        cg = csum[:, :, g]
        shifted = jnp.pad(cg, ((0, 0), (win, 0), (0, 0)))[:, :S]
        count = jnp.minimum(pos + 1, win).astype(jnp.float32)
        outs.append((cg - shifted) / count[None, :, None] - ug[:, :, g])
    y = jnp.stack(outs, axis=2).astype(u.dtype)
    y = jnp.einsum('bsgc,gcd->bsgd', y, w_pool).reshape(B, S, POOL_WIDTH)
    return y * pool_scale

def conformer_conv(val, gate, conv_w, conv_b, ln_g, ln_b):
    u = val * jax.nn.sigmoid(gate)
    y = lax.conv_general_dilated(
        u, conv_w[:, None, :].astype(u.dtype), window_strides=(1,),
        padding=[(CONV_KERNEL - 1, 0)],
        dimension_numbers=('NWC', 'WIO', 'NWC'),
        feature_group_count=CONV_WIDTH) + conv_b
    y = layernorm(y, ln_g, ln_b)
    return jax.nn.silu(y)

def hybrid_mixer(h, w_in, pool_w, pool_scale, conv_w, conv_b, ln_g, ln_b, gn_g, w_out):
    B, S, _ = h.shape
    p = h @ w_in
    a0 = ATTN_WIDTH
    q, k, v, u_pool, c_val, c_gate = jnp.split(
        p, [a0, 2 * a0, 3 * a0, 3 * a0 + POOL_WIDTH, 3 * a0 + POOL_WIDTH + CONV_WIDTH], axis=-1)
    shp = (B, S, N_SB_HEADS, SB_HEAD_DIM)
    o_a = stick_breaking_attention(q.reshape(shp), k.reshape(shp), v.reshape(shp)).reshape(B, S, ATTN_WIDTH)
    o_b = multiscale_pool(u_pool, pool_w, pool_scale)
    o_c = conformer_conv(c_val, c_gate, conv_w, conv_b, ln_g, ln_b)
    g_a, g_b, g_c = jnp.split(gn_g, [ATTN_WIDTH, ATTN_WIDTH + POOL_WIDTH])
    o = jnp.concatenate([rmsnorm(o_a, g_a), rmsnorm(o_b, g_b), rmsnorm(o_c, g_c)], axis=-1)
    return o @ w_out

def swiglu(h, w_gate, w_up, w_down):
    return (jax.nn.silu(h @ w_gate) * (h @ w_up)) @ w_down

def moe_swiglu(h, w_router, w_gate, w_up, w_down):
    B, S, D = h.shape
    t = h.reshape(B * S, D)
    logits = (t @ w_router).astype(jnp.float32)
    top_v, top_i = lax.top_k(logits, TOP_K)
    gates = jax.nn.softmax(top_v, axis=-1)
    combine = jnp.sum(jax.nn.one_hot(top_i, N_EXPERTS, dtype=jnp.float32) * gates[..., None], axis=1)
    combine = combine.astype(h.dtype)
    out = jnp.zeros_like(t)
    for e in range(N_EXPERTS):
        out = out + combine[:, e:e + 1] * swiglu(t, w_gate[e], w_up[e], w_down[e])
    return out.reshape(B, S, D)

def setup_inputs(seed: int = 0) -> dict:
    key = jax.random.key(seed)
    ks = jax.random.split(key, 24)
    f32 = jnp.float32

    def nrm(k, shape, scale):
        return jax.random.normal(k, shape, f32) * scale

    def gain(k, shape):
        return 1.0 + 0.02 * jax.random.normal(k, shape, f32)

    return {
        "x": nrm(ks[0], (BATCH, SEQ, D_MODEL), 1.0),
        "attn_norm_g": gain(ks[1], (DEPTH, D_MODEL)),
        "w_in": nrm(ks[2], (DEPTH, D_MODEL, IN_COLS), D_MODEL ** -0.5),
        "pool_w": nrm(ks[3], (DEPTH, N_POOL_GROUPS, POOL_GROUP_DIM, POOL_GROUP_DIM), POOL_GROUP_DIM ** -0.5),
        "pool_scale": gain(ks[4], (DEPTH, POOL_WIDTH)),
        "conv_w": nrm(ks[5], (DEPTH, CONV_KERNEL, CONV_WIDTH), CONV_KERNEL ** -0.5),
        "conv_b": nrm(ks[6], (DEPTH, CONV_WIDTH), 0.02),
        "conv_ln_g": gain(ks[7], (DEPTH, CONV_WIDTH)),
        "conv_ln_b": nrm(ks[8], (DEPTH, CONV_WIDTH), 0.02),
        "group_norm_g": gain(ks[9], (DEPTH, D_MIX)),
        "w_out": nrm(ks[10], (DEPTH, D_MIX, D_MODEL), D_MIX ** -0.5),
        "ffn_norm_g": gain(ks[11], (DEPTH, D_MODEL)),
        "dense_w_gate": nrm(ks[12], (N_DENSE, D_MODEL, D_FF), D_MODEL ** -0.5),
        "dense_w_up": nrm(ks[13], (N_DENSE, D_MODEL, D_FF), D_MODEL ** -0.5),
        "dense_w_down": nrm(ks[14], (N_DENSE, D_FF, D_MODEL), D_FF ** -0.5),
        "router_w": nrm(ks[15], (N_MOE, D_MODEL, N_EXPERTS), D_MODEL ** -0.5),
        "moe_w_gate": nrm(ks[16], (N_MOE, N_EXPERTS, D_MODEL, D_FF), D_MODEL ** -0.5),
        "moe_w_up": nrm(ks[17], (N_MOE, N_EXPERTS, D_MODEL, D_FF), D_MODEL ** -0.5),
        "moe_w_down": nrm(ks[18], (N_MOE, N_EXPERTS, D_FF, D_MODEL), D_FF ** -0.5),
        "final_norm_g": gain(ks[19], (D_MODEL,)),
    }

def reference(x, attn_norm_g, w_in, pool_w, pool_scale, conv_w, conv_b, conv_ln_g, conv_ln_b,
              group_norm_g, w_out, ffn_norm_g, dense_w_gate, dense_w_up, dense_w_down,
              router_w, moe_w_gate, moe_w_up, moe_w_down, final_norm_g):
    for l in range(DEPTH):
        h = rmsnorm(x, attn_norm_g[l])
        x = x + hybrid_mixer(h, w_in[l], pool_w[l], pool_scale[l], conv_w[l], conv_b[l],
                             conv_ln_g[l], conv_ln_b[l], group_norm_g[l], w_out[l])
        h = rmsnorm(x, ffn_norm_g[l])
        if l % 2 == 0:
            i = l // 2
            x = x + swiglu(h, dense_w_gate[i], dense_w_up[i], dense_w_down[i])
        else:
            i = l // 2
            x = x + moe_swiglu(h, router_w[i], moe_w_gate[i], moe_w_up[i], moe_w_down[i])
    return rmsnorm(x, final_norm_g)


_drawn_inputs = setup_inputs


def setup_inputs(seed=0):
    import zlib

    import numpy as np

    out = dict(_drawn_inputs(seed))
    spreads = {}
    factors = {'pool_scale': 28.25, 'conv_ln_g': 23.921, 'conv_ln_b': 28.152, 'final_norm_g': 22.978}
    for name, (base, spread) in spreads.items():
        noise = np.random.default_rng([zlib.crc32(name.encode()), seed]).standard_normal(out[name].shape)
        drawn = base * np.exp(spread * noise) if base else spread * noise
        out[name] = __import__('jax').numpy.asarray(drawn.astype(out[name].dtype))
    for name, factor in factors.items():
        out[name] = (out[name] * factor).astype(out[name].dtype)
    return out
```

```python
from contextlib import ExitStack

import numpy as np

import concourse.bass as bass
from concourse import mybir

ALU = mybir.AluOpType
ACT = mybir.ActivationFunctionType
AX = mybir.AxisListType.X
F32 = mybir.dt.float32
F32R = mybir.dt.float32r
BF16 = mybir.dt.bfloat16
I32 = mybir.dt.int32

P = 128
DEPTH = 2
T = 256
NT = T // P
D = 1024
KD = D // P
ATTN = 512
HEADS = 8
HD = 64
POOL = 256
WINDOWS = (2, 4, 8, 16)
CONV = 256
CH = CONV // P
TAPS = 31
IN_COLS = 3 * ATTN + POOL + 2 * CONV
F = 2816
UF = 256
UNITS = F // UF
E = 8
CAP = 128
EXTRA = 3
JOBCOLS = E + EXTRA + 1
RMS_EPS = 1e-6
LN_EPS = 1e-5
BIG = 1e30
LOWEST = -3e38
Z = T + P

W_IN_BLOCKS = 9
W_OUT_BLOCKS = 4
MIX_BLOCKS = W_IN_BLOCKS + W_OUT_BLOCKS
FFN_BLOCKS = 3 * UNITS
LAYER_BLOCKS = MIX_BLOCKS + FFN_BLOCKS
RAW = 9
AHEAD = 6
HEAD_SLOTS = (6, 7)
TAIL_SLOT = 8
PAIRS = (UNITS - 3) // 2
LOADS = (UNITS - 1) // 2
FILL = 32

PROJ = [(0, 8, 3 * ATTN + POOL + CONV, CONV)]
for first in (3 * ATTN, 0, ATTN, 2 * ATTN):
    PROJ += [(0, 4, first, 512), (4, 4, first, 512)]

C_ID, C_MASK, C_NEG = 0, P, P + Z
C_TRIN = C_NEG + Z
C_ONEN = C_TRIN + P
C_POOL = C_ONEN + P
C_RANK = C_POOL + len(WINDOWS) * Z
C_ONE = C_RANK + P
C_IOTA = C_ONE + P
C_REV = C_IOTA + P
C_TRIE = C_REV + E
C_OIDX = C_TRIE + E * E
C_EIDX = C_OIDX + EXTRA * E
C_ONECOL = C_EIDX + E
C_COLS = C_ONECOL + 1

R_GAP, R_EXP, R_MASK, R_GATES, R_COLS = 18, 20, 96, 348, 384

Q_ATTN_G, Q_FFN_G, Q_GN_G = 0, KD, 2 * KD
Q_CONV_W = 3 * KD
Q_CONV_B = Q_CONV_W + CH * TAPS
Q_POOL_W = Q_CONV_B + CH
Q_POOL_S = Q_POOL_W + 2 * HD
Q_LN_G = Q_POOL_S + POOL
Q_LN_B = Q_LN_G + CONV
Q_COLS = Q_LN_B + CONV


def constants():
    c = np.zeros((P, C_COLS), np.float32)
    p = np.arange(P)[:, None]
    col = np.arange(P)[None, :]
    c[:, C_ID:C_ID + P] = p == col
    t = np.concatenate([np.arange(T), np.arange(P, T)])[None, :]
    s = np.concatenate([np.zeros(T), np.full(P, P)])[None, :] + p
    c[:, C_MASK:C_MASK + Z] = s < t
    c[:, C_NEG:C_NEG + Z] = np.where(s < t, 0.0, -BIG)
    c[:, C_TRIN:C_TRIN + P] = np.where(p >= col, -1.0, 0.0)
    c[:, C_ONEN:C_ONEN + P] = -1.0
    for g, w in enumerate(WINDOWS):
        count = np.minimum(t + 1, w)
        c[:, C_POOL + g * Z:C_POOL + (g + 1) * Z] = np.where((s <= t) & (s > t - w), 1.0 / count, 0.0) - (s == t)
    c[:, C_RANK:C_RANK + P] = p < col
    c[:, C_ONE:C_ONE + P] = 1.0
    c[:, C_IOTA:C_IOTA + P] = col
    c[:, C_REV:C_REV + E] = E - np.arange(E)
    c[:, C_TRIE:C_TRIE + E * E] = (np.arange(E)[None, :] < np.arange(E)[:, None]).reshape(1, -1)
    c[:, C_OIDX:C_OIDX + EXTRA * E] = np.repeat(np.arange(EXTRA), E)[None, :]
    c[:, C_EIDX:C_EIDX + E] = np.arange(E)
    c[:, C_ONECOL] = 1.0
    return c


def raw_slot(i):
    return HEAD_SLOTS[0] if i == 0 else (i - 1) % 6


def build(nc, x, w_in, w_out, dense_gate, dense_up, dense_down, moe_gate, moe_up, moe_down, params, router, moe_g,
          final_g, consts, out):
    with ExitStack() as ctx:
        def sb(name, shape, dt=F32):
            return ctx.enter_context(nc.sbuf_tensor(name, shape, dt))

        def sem(name):
            return ctx.enter_context(nc.semaphore(name))

        cst = sb("cst", [P, C_COLS])
        prm = sb("prm", [P, DEPTH, Q_COLS])
        rw32 = sb("rw32", [P, KD * E])
        raw = sb("raw", [P, RAW, 2048])
        whi = sb("whi", [P, 3, 2048], F32R)
        wlo = sb("wlo", [P, 3, 2048], F32R)
        xs = sb("xs", [P, NT, D])
        nat = sb("nat", [P, NT, D])
        xT_hi = sb("xT_hi", [P, KD, T], F32R)
        xT_lo = sb("xT_lo", [P, KD, T], F32R)
        hid = sb("hid", [P, 2, NT, UF])
        hs, hn = hid[:, 0], hid[:, 1]
        junk = hid[:, :, :, :].rearrange("p a t c -> p (a t c)")
        hT_hi = sb("hT_hi", [P, 2, T], F32R)
        hT_lo = sb("hT_lo", [P, 2, T], F32R)
        zeros = sb("zeros", [P, P], BF16)
        st = sb("st", [P, 64])
        jobs = sb("jobs", [P, 1 + EXTRA], I32)

        with ExitStack() as mixers:
            def mixer_sb(name, shape):
                return mixers.enter_context(nc.sbuf_tensor(name, shape, F32))

            qT = mixer_sb("qT", [P, ATTN // P, T])
            kT = mixer_sb("kT", [P, ATTN // P, T])
            vn = mixer_sb("vn", [P, NT, ATTN])
            wgt = mixer_sb("wgt", [P, 2, Z])
            up_n = mixer_sb("up_n", [P, NT, POOL])
            sig = mixer_sb("sig", [P, CH, T])
            uT = mixer_sb("uT", [P, CH, TAPS - 1 + T])
            cT = mixer_sb("cT", [P, CH, T])
            cn = mixer_sb("cn", [P, NT, CONV])
        ob = sig
        flat = nat[:, :, :].rearrange("p t d -> p (t d)")
        lnb = flat[:, 0:2 * Z].rearrange("p (b z) -> p b z", b=2)
        sp_b = flat[:, 2 * Z:4 * Z].rearrange("p (b z) -> p b z", b=2)
        yT = flat[:, 4 * Z:4 * Z + 2 * T].rearrange("p (g t) -> p g t", g=2)

        xn_hi = sb("xn_hi", [P, NT, D], F32R)
        xn_lo = sb("xn_lo", [P, NT, D], F32R)
        rw_hi = sb("rw_hi", [P, KD * E], F32R)
        rw_lo = sb("rw_lo", [P, KD * E], F32R)
        hot = sb("hot", [P, NT, CAP], F32R)
        hotT = sb("hotT", [P, T], F32R)
        slot_gate = sb("slot_gate", [P, 1])
        rt = sb("rt", [P, R_COLS])
        row_g = sb("row_g", [P, D])
        bank = [ctx.enter_context(nc.psum_tensor(f"bank{b}", [P, 512], F32)) for b in range(8)]

        ident = cst[:, C_ID:C_ID + P]
        mask = cst[:, C_MASK:C_MASK + Z]
        negm = cst[:, C_NEG:C_NEG + Z]
        xeT_hi, xeT_lo = xT_hi[:, :, 0:CAP], xT_lo[:, :, 0:CAP]
        y_hi, y_lo = xT_hi[:, :, CAP:T], xT_lo[:, :, CAP:T]

        x_landed, c_landed, p_landed = (sem(n) for n in ("x_landed", "c_landed", "p_landed"))
        moe_g_landed, final_g_landed = sem("moe_g_landed"), sem("final_g_landed")
        slot_landed = [sem(f"slot_landed{s}") for s in range(RAW)]
        split_hi, split_lo, blocks_used = sem("split_hi"), sem("split_lo"), sem("blocks_used")
        sumsq_done = sem("sumsq_done")
        var_ready, ln_done, rsqrt_rough = sem("var_ready"), sem("ln_done"), sem("rsqrt_rough")
        nat_ready, turned, xT_hi_ready, xT_lo_ready = sem("nat_ready"), sem("turned"), sem("xT_hi_ready"), sem("xT_lo_ready")
        gate_sig, conv_in, pool_in, q_in, k_in, v_in = (sem(n) for n in ("gate_sig", "conv_in", "pool_in", "q_in", "k_in", "v_in"))
        z_ready, abs_done, exp_done, ln_ready = sem("z_ready"), sem("abs_done"), sem("exp_done"), sem("ln_ready")
        sp_raw, sp_ready, c_ready, arg_ready, w_ready, pv_done = (
            sem(n) for n in ("sp_raw", "sp_ready", "c_ready", "arg_ready", "w_ready", "pv_done"))
        pool_mixed, yT_ready, pool_done = sem("pool_mixed"), sem("yT_ready"), sem("pool_done")
        padded, conv_step, conv_turned = sem("padded"), sem("conv_step"), sem("conv_turned")
        group_in, lin_ready, swish_done = sem("group_in"), sem("lin_ready"), sem("swish_done")
        table_ready = sem("table_ready")
        x_updated, silu_ready, h_ready = sem("x_updated"), sem("silu_ready"), sem("h_ready")
        h_turned, hT_hi_ready, hT_lo_ready = sem("h_turned"), sem("hT_hi_ready"), sem("hT_lo_ready")
        xn_hi_ready, xn_lo_ready, rw_hi_ready, rw_lo_ready = (sem(n) for n in ("xn_hi_ready", "xn_lo_ready", "rw_hi_ready", "rw_lo_ready"))
        logits_ready, gap_ready, gap_exp, mask_ready, rank_ready = (
            sem(n) for n in ("logits_ready", "gap_ready", "gap_exp", "mask_ready", "rank_ready"))
        route_ready, hot_ready, gathered, xe_hi_ready, xe_lo_ready = (
            sem(n) for n in ("route_ready", "hot_ready", "gathered", "xe_hi_ready", "xe_lo_ready"))
        y_hi_ready, y_lo_ready, scattered, added = sem("y_hi_ready"), sem("y_lo_ready"), sem("scattered"), sem("added")
        hot_turned, hotT_ready = sem("hot_turned"), sem("hotT_ready")
        dve_step, out_done, out_landed = sem("dve_step"), sem("out_done"), sem("out_landed")

        def layer_base(l):
            return l * LAYER_BLOCKS

        class Dense:
            tiles = NT
            base = MIX_BLOCKS
            unit0 = 0
            gu0 = 0
            parts = 0
            loop_fills, head_fills, tail_fills = 2, 1, 0
            acc = (3, 4, 5, 6)

        def job_part(j):
            class Job:
                tiles = 1
                base = layer_base(1) + MIX_BLOCKS + FFN_BLOCKS * j
                unit0 = UNITS + UNITS * j
                gu0 = NT * UNITS + UNITS * j
                parts = 1 + j
                loop_fills, head_fills, tail_fills = 4 + LOADS + LOADS * j, 3 + j, 1 + j
                acc = (3, 4)
            return Job

        def buf(part, pos):
            return ((MIX_BLOCKS if part.tiles == NT else layer_base(1) + MIX_BLOCKS) + pos) % 3

        def mixer_fill(l, i):
            if i == 0:
                return 1 if l == 0 else 3
            return (0 if l == 0 else 2 + LOADS) + (i - 1) // 6 + 1

        block = ctx.enter_context(nc.Block())

        @block.sync
        def _(sp):
            def load(n, slot, pieces):
                if not (isinstance(n, int) and n < AHEAD):
                    sp.wait_ge(split_lo, n - AHEAD + 1)
                for dst, src in pieces:
                    sp.dma_start(dst, src).then_inc(slot_landed[slot], 16)

            def rows(w, k0, nk, c0, ncols):
                return w[k0 * P:(k0 + nk) * P, c0:c0 + ncols].rearrange("(k p) c -> p k c", p=P)

            def mixer_block(l, i):
                w, (k0, nk, c0, ncols) = (w_in[l], PROJ[i]) if i < W_IN_BLOCKS else (
                    w_out[l], (4 * ((i - W_IN_BLOCKS) % 2), 4, 512 * ((i - W_IN_BLOCKS) // 2), 512))
                s = raw_slot(i)
                dst = raw[:, s, :].rearrange("p (k c) -> p k c", k=nk)
                h = nk // 2
                load(layer_base(l) + i, s, [(dst[:, 0:h], rows(w, k0, h, c0, ncols)),
                                            (dst[:, h:nk], rows(w, k0 + h, h, c0, ncols))])

            def gate_up(part, wg, wu, pos, half, i, slot):
                dst = raw[:, slot, :].rearrange("p (k g c) -> p k g c", k=4, g=2)
                src = [w[half * 512:(half + 1) * 512, bass.ds(i * UF, UF)].rearrange("(k p) c -> p k c", p=P)
                       for w in (wg, wu)]
                load(part.base + pos, slot, [(dst[:, :, g, :], src[g]) for g in range(2)])

            def down(part, wd, pos, i, slot):
                dst = raw[:, slot, :].rearrange("p (k c) -> p k c", k=2)
                load(part.base + pos, slot, [(dst[:, k, :], wd[bass.ds(i * UF + k * P, P), :]) for k in range(2)])

            def ffn(part, wg, wu, wd):
                gate_up(part, wg, wu, 0, 0, 0, HEAD_SLOTS[0])
                gate_up(part, wg, wu, 1, 1, 0, HEAD_SLOTS[1])
                with sp.Fori(0, LOADS) as k:
                    for u in range(2):
                        i = 2 * k + 1 + u
                        pos = 2 + 6 * k + 3 * u
                        gate_up(part, wg, wu, pos, 0, i, 3 * u)
                        gate_up(part, wg, wu, pos + 1, 1, i, 3 * u + 1)
                        down(part, wd, pos + 2, i - 1, 3 * u + 2)
                down(part, wd, FFN_BLOCKS - 1, UNITS - 1, TAIL_SLOT)

            sp.dma_start(xs[:, :, :], x[0].rearrange("(t p) d -> p t d", p=P)).then_inc(x_landed, 16)
            sp.dma_start(cst[:, :], consts).then_inc(c_landed, 16)
            sp.dma_start(prm[:, :, :], params).then_inc(p_landed, 16)
            sp.dma_start(rw32[:, :], router).then_inc(p_landed, 16)
            for i in range(MIX_BLOCKS):
                mixer_block(0, i)
            ffn(Dense, dense_gate[0], dense_up[0], dense_down[0])
            for i in range(MIX_BLOCKS):
                mixer_block(1, i)
            with sp.Fori(0, E) as j:
                ffn(job_part(j), moe_gate[0, j], moe_up[0, j], moe_down[0, j])
            sp.wait_ge(route_ready, 1)
            sp.dma_start(row_g[:, :], final_g).then_inc(final_g_landed, 16)
            njobs = sp.value_load(jobs[0:1, 0:1], min_val=E, max_val=E + EXTRA)
            with sp.If(njobs > E):
                with sp.Fori(E, njobs) as j:
                    e = sp.value_load(jobs[0:1, bass.ds(j - (E - 1), 1)], min_val=0, max_val=E - 1)
                    ffn(job_part(j), moe_gate[0, e], moe_up[0, e], moe_down[0, e])
            for t in range(NT):
                sp.wait_ge(out_done, t + 1)
                sp.dma_start(out[0, t * P:(t + 1) * P, :], nat[:, t, :]).then_inc(out_landed, 16)
            sp.wait_ge(out_landed, 16 * NT)

        @block.gpsimd
        def _(pool):
            pool.memset(uT[:, :, :], 0.0).then_inc(padded, 1)
            pool.memset(zeros[:, :], 0.0).then_inc(padded, 1)
            pool.wait_ge(nat_ready, 10)
            pool.dma_start(row_g[:, :], moe_g).then_inc(moe_g_landed, 16)

        @block.scalar
        def _(act):
            def hi(n, slot, fill, b):
                act.wait_ge(slot_landed[slot], FILL * fill)
                if not (isinstance(n, int) and n < 3):
                    act.wait_ge(blocks_used, n - 2)
                act.activation(whi[:, b, :], raw[:, slot, :], ACT.Copy).then_inc(split_hi, 1)

            def mixer_hi(l, i):
                n = layer_base(l) + i
                hi(n, raw_slot(i), mixer_fill(l, i), n % 3)

            def rsqrt(m, cols, c0):
                act.wait_ge(var_ready, m + 1)
                act.activation(st[:, c0 + 16:c0 + 16 + cols], st[:, c0:c0 + cols], ACT.Ln).then_inc(ln_done, 1)
                act.wait_ge(ln_done, m + 1)
                act.activation(st[:, c0 + 32:c0 + 32 + cols], st[:, c0 + 16:c0 + 16 + cols], ACT.Exp, scale=-0.5)\
                    .then_inc(rsqrt_rough, 1)

            def sum_squares(src, width, c, n):
                if n > 1:
                    act.wait_ge(sumsq_done, n - 1)
                act.activation(junk[:, 0:width], src, ACT.Square, accum_out=st[:, c:c + 1]).then_inc(sumsq_done, 1)

            def turn_hi(e, gcol, l):
                for b in range(4):
                    act.wait_ge(turned, 4 * e + b + 1)
                    if gcol is None:
                        act.activation(xT_hi[:, 2 * b:2 * b + 2, :], bank[turn_banks(e)[b]][:, :]
                                       .rearrange("p (k t) -> p k t", k=2), ACT.Copy).then_inc(xT_hi_ready, 2)
                        continue
                    for k in (2 * b, 2 * b + 1):
                        act.activation(xT_hi[:, k, :], bank[turn_banks(e)[b]][:, (k % 2) * T:(k % 2 + 1) * T], ACT.Copy,
                                       scale=prm[:, l, gcol + k:gcol + k + 1]).then_inc(xT_hi_ready, 1)

            def silu(part, i, u):
                act.wait_ge(blocks_used, part.base + gate_up_pos(i) + 1)
                for t in range(part.tiles):
                    act.activation(hs[:, t, :], bank[gu_bank(part, t, u)][:, 0:UF], ACT.Silu).then_inc(silu_ready, 1)

            def hT_hi_copy(part, i):
                w = part.tiles * P
                act.wait_ge(h_turned, part.unit0 + i + 1)
                act.activation(hT_hi[:, :, 0:w], bank[2][:, 0:2 * w].rearrange("p (f t) -> p f t", f=2), ACT.Copy)\
                    .then_inc(hT_hi_ready, 1)

            def unit(part, i, u, fill, between=None):
                pos = 3 * i - 1
                hi(part.base + pos, 3 * u, fill, buf(part, 2))
                if between:
                    between()
                hi(part.base + pos + 1, 3 * u + 1, fill, buf(part, 3))
                silu(part, i - 1, u)
                hi(part.base + pos + 2, 3 * u + 2, fill, buf(part, 4))
                hT_hi_copy(part, i - 1)

            def units(part, between=None):
                unit(part, 1, 0, part.loop_fills + 1, between)
                with act.Fori(0, PAIRS) as k:
                    for u in (1, 0):
                        unit(part, 2 * k + 3 - u, u, part.loop_fills + k + 2 - u)
                unit(part, UNITS - 1, 1, part.loop_fills + PAIRS + 1)
                hi(part.base + FFN_BLOCKS - 1, TAIL_SLOT, part.tail_fills + 1, buf(part, FFN_BLOCKS - 1))
                silu(part, UNITS - 1, 0)
                hT_hi_copy(part, UNITS - 1)

            def y_hi_copy(done):
                act.wait_ge(blocks_used, job_part(done).base)
                act.wait_ge(hotT_ready, done + 1)
                for n in range(2):
                    act.activation(y_hi[:, 4 * n:4 * n + 4, :], bank[3 + n][:, :].rearrange("p (k c) -> p k c", k=4),
                                   ACT.Copy, scale=slot_gate[:, 0:1]).then_inc(y_hi_ready, 1)

            def load_exp_and_ln():
                act.preload_act_table_set("natural_log_exp_and_others")

            norms = 0
            sums = 0
            for l in range(DEPTH):
                load_exp_and_ln()
                for i in range(3):
                    mixer_hi(l, i)
                if l == 0:
                    act.wait_ge(x_landed, 16)
                    act.wait_ge(p_landed, 32)
                else:
                    act.wait_ge(x_updated, 8 * l)
                for t in range(NT):
                    sums += 1
                    sum_squares(xs[:, t, :], D, 48 + t, sums)
                rsqrt(norms, 2, 0)
                norms += 1
                turn_hi(3 * l, Q_ATTN_G, l)
                mixer_hi(l, 3)
                act.wait_ge(blocks_used, layer_base(l) + 1)
                act.activation(sig[:, :, :], bank[0][:, :].rearrange("p (h t) -> p h t", h=CH), ACT.Sigmoid)\
                    .then_inc(gate_sig, 1)
                load_exp_and_ln()
                mixer_hi(l, 4)
                mixer_hi(l, 5)
                act.wait_ge(blocks_used, layer_base(l) + 3)
                act.activation(up_n[:, :, :], bank[1][:, :].rearrange("p (t c) -> p t c", t=NT), ACT.Copy)\
                    .then_inc(pool_in, 1)
                mixer_hi(l, 6)
                mixer_hi(l, 7)
                act.wait_ge(blocks_used, layer_base(l) + 5)
                for b in range(2):
                    act.activation(qT[:, 2 * b:2 * b + 2, :], bank[3 + b][:, :].rearrange("p (c t) -> p c t", c=2),
                                   ACT.Copy, scale=HD ** -0.5).then_inc(q_in, 1)
                for i in range(8, 12):
                    mixer_hi(l, i)
                act.wait_ge(blocks_used, layer_base(l) + 9)
                for t in range(NT):
                    act.activation(vn[:, t, :], bank[(0, 7)[t]][:, :], ACT.Copy).then_inc(v_in, 1)

                for h in range(HEADS + 1):
                    n = HEADS * l + h
                    if h < HEADS:
                        zb = bank[1 + h % 3]
                        act.wait_ge(z_ready, n + 1)
                        if n >= 2:
                            act.wait_ge(sp_raw, n - 1)
                        act.activation(lnb[:, h % 2, :], zb[:, 0:Z], ACT.Abs).then_inc(abs_done, 1)
                        act.wait_ge(abs_done, n + 1)
                        act.activation(lnb[:, h % 2, :], lnb[:, h % 2, :], ACT.Exp, scale=-1.0).then_inc(exp_done, 1)
                        act.wait_ge(exp_done, n + 1)
                        act.activation(lnb[:, h % 2, :], lnb[:, h % 2, :], ACT.Ln, bias=cst[:, C_ONECOL:C_ONECOL + 1])\
                            .then_inc(ln_ready, 1)
                    if h >= 1:
                        act.wait_ge(arg_ready, n)
                        g = (h - 1) % 2
                        act.activation(wgt[:, g, :], wgt[:, g, :], ACT.Exp).then_inc(w_ready, 1)
                act.wait_ge(pv_done, HEADS * (l + 1))
                for t in range(NT):
                    sums += 1
                    sum_squares(bank[4 + t][:, :], ATTN, 50 + t, sums)
                act.wait_ge(group_in, 2 * l + 1)
                for t in range(NT):
                    sums += 1
                    sum_squares(ob[:, t, :], POOL, 52 + t, sums)
                act.wait_ge(group_in, 2 * l + 2)
                for t in range(NT):
                    sums += 1
                    sum_squares(cn[:, t, :], CONV, 54 + t, sums)
                rsqrt(norms, 2, 0)
                norms += 1
                act.wait_ge(lin_ready, l + 1)
                act.activation(cn[:, :, :], cn[:, :, :], ACT.Silu).then_inc(swish_done, 1)
                load_exp_and_ln()
                act.wait_ge(swish_done, l + 1)
                for t in range(NT):
                    sums += 1
                    sum_squares(cn[:, t, :], CONV, 54 + t, sums)
                rsqrt(norms, 6, 0)
                norms += 1
                turn_hi(3 * l + 1, Q_GN_G, l)
                mixer_hi(l, 12)
                if l == 0:
                    hi(Dense.base, HEAD_SLOTS[0], Dense.head_fills + 1, buf(Dense, 0))
                    hi(Dense.base + 1, HEAD_SLOTS[1], Dense.tail_fills + 1, buf(Dense, 1))
                act.wait_ge(x_updated, 8 * l + 4)
                for t in range(NT):
                    sums += 1
                    sum_squares(xs[:, t, :], D, 48 + t, sums)
                rsqrt(norms, 2, 0)
                norms += 1
                if l == 1:
                    act.activation(rw_hi[:, :], rw32[:, :], ACT.Copy).then_inc(rw_hi_ready, 1)
                    act.wait_ge(nat_ready, 12)
                    act.activation(xn_hi[:, :, :], nat[:, :, :], ACT.Copy).then_inc(xn_hi_ready, 1)
                turn_hi(3 * l + 2, Q_FFN_G if l == 0 else None, l)
                if l == 0:
                    act.activation(st[:, 60:61], cst[:, C_ONECOL:C_ONECOL + 1], ACT.Silu).then_inc(table_ready, 1)
                    units(Dense)
            act.wait_ge(gap_ready, 1)
            act.activation(rt[:, R_EXP:R_EXP + NT], rt[:, R_GAP:R_GAP + NT], ACT.Exp).then_inc(gap_exp, 1)
            act.wait_ge(table_ready, 1)
            act.activation(st[:, 60:61], cst[:, C_ONECOL:C_ONECOL + 1], ACT.Silu).then_inc(table_ready, 1)
            act.wait_ge(route_ready, 1)
            njobs = act.value_load(jobs[0:1, 0:1], min_val=E, max_val=E + EXTRA)
            with act.Fori(0, njobs) as j:
                part = job_part(j)
                hi(part.base, HEAD_SLOTS[0], part.head_fills + 1, buf(part, 0))
                for b in range(2):
                    act.wait_ge(gathered, 2 * j + b + 1)
                    act.activation(xeT_hi[:, 4 * b:4 * b + 4, :], bank[5 + b][:, :].rearrange("p (k c) -> p k c", k=4),
                                   ACT.Copy).then_inc(xe_hi_ready, 1)
                hi(part.base + 1, HEAD_SLOTS[1], part.tail_fills + 1, buf(part, 1))
                units(part, lambda: y_hi_copy(j))
            load_exp_and_ln()
            y_hi_copy(njobs)
            act.wait_ge(added, 4 * njobs + 4)
            for t in range(NT):
                sums += 1
                sum_squares(xs[:, t, :], D, 48 + t, sums)
            rsqrt(norms, 2, 0)

        @block.vector
        def _(dve):
            steps = [0]

            def link(ins):
                steps[0] += 1
                ins.then_inc(dve_step, 1)
                dve.wait_ge(dve_step, steps[0])

            def lo(n, slot, b):
                dve.wait_ge(split_hi, n + 1)
                dve.tensor_tensor(wlo[:, b, :], raw[:, slot, :], whi[:, b, :].bitcast(F32), ALU.subtract)\
                    .then_inc(split_lo, 1)

            def mixer_lo(l, i):
                n = layer_base(l) + i
                lo(n, raw_slot(i), n % 3)

            def newton(m, cols, c0):
                v, y, u = (st[:, a:a + cols] for a in (c0, c0 + 32, c0 + 16))
                dve.wait_ge(rsqrt_rough, m + 1)
                link(dve.tensor_tensor(u, y, y, ALU.mult))
                link(dve.tensor_tensor(u, u, v, ALU.mult))
                link(dve.tensor_scalar(u, u, -0.5, 1.5, ALU.mult, ALU.add))
                link(dve.tensor_tensor(y, y, u, ALU.mult))

            def norm_rows(m, sums, gains=None):
                dve.wait_ge(sumsq_done, sums)
                dve.tensor_scalar(st[:, 0:2], st[:, 48:50], 1.0 / D, RMS_EPS, ALU.mult, ALU.add).then_inc(var_ready, 1)
                dve.wait_ge(var_ready, m + 1)
                newton(m, 2, 0)
                for t in range(NT):
                    if gains is None:
                        ins = dve.tensor_scalar(nat[:, t, :], xs[:, t, :], st[:, 32 + t:33 + t], None, ALU.mult)
                    else:
                        ins = dve.scalar_tensor_tensor(nat[:, t, :], xs[:, t, :], st[:, 32 + t:33 + t], gains,
                                                       ALU.mult, ALU.mult)
                    ins.then_inc(nat_ready, 1)

            def turn_lo(e, gcol, l):
                for b in range(4):
                    dve.wait_ge(xT_hi_ready, 8 * e + 2 * b + 2)
                    if gcol is None:
                        dve.tensor_tensor(xT_lo[:, 2 * b:2 * b + 2, :], bank[turn_banks(e)[b]][:, :]
                                          .rearrange("p (k t) -> p k t", k=2), xT_hi[:, 2 * b:2 * b + 2, :].bitcast(F32),
                                          ALU.subtract).then_inc(xT_lo_ready, 2)
                        continue
                    for k in (2 * b, 2 * b + 1):
                        dve.scalar_tensor_tensor(xT_lo[:, k, :], bank[turn_banks(e)[b]][:, (k % 2) * T:(k % 2 + 1) * T],
                                                 prm[:, l, gcol + k:gcol + k + 1], xT_hi[:, k, :].bitcast(F32),
                                                 ALU.mult, ALU.subtract).then_inc(xT_lo_ready, 1)

            def gated(part, i, u):
                for t in range(part.tiles):
                    dve.wait_ge(silu_ready, part.gu0 + part.tiles * i + t + 1)
                    dve.tensor_tensor(hn[:, t, :], bank[gu_bank(part, t, u)][:, UF:2 * UF], hs[:, t, :], ALU.mult)\
                        .then_inc(h_ready, 1)

            def hT_lo_copy(part, i):
                w = part.tiles * P
                dve.wait_ge(hT_hi_ready, part.unit0 + i + 1)
                dve.tensor_tensor(hT_lo[:, :, 0:w], bank[2][:, 0:2 * w].rearrange("p (f t) -> p f t", f=2),
                                  hT_hi[:, :, 0:w].bitcast(F32), ALU.subtract).then_inc(hT_lo_ready, 1)

            def unit(part, i, u, between=None):
                pos = 3 * i - 1
                lo(part.base + pos, 3 * u, buf(part, 2))
                if between:
                    between()
                    gated(part, i - 1, u)
                    lo(part.base + pos + 1, 3 * u + 1, buf(part, 3))
                else:
                    lo(part.base + pos + 1, 3 * u + 1, buf(part, 3))
                    gated(part, i - 1, u)
                lo(part.base + pos + 2, 3 * u + 2, buf(part, 4))
                hT_lo_copy(part, i - 1)

            def units(part, between=None, after_unit1=None, before_last=None):
                unit(part, 1, 0, between)
                if after_unit1:
                    after_unit1()
                with dve.Fori(0, PAIRS) as k:
                    for u in (1, 0):
                        unit(part, 2 * k + 3 - u, u)
                if before_last:
                    before_last()
                unit(part, UNITS - 1, 1)
                lo(part.base + FFN_BLOCKS - 1, TAIL_SLOT, buf(part, FFN_BLOCKS - 1))
                gated(part, UNITS - 1, 0)
                hT_lo_copy(part, UNITS - 1)

            def add_to_x(t, n, b, s):
                dve.tensor_tensor(xs[:, t, n * 512:(n + 1) * 512], xs[:, t, n * 512:(n + 1) * 512], bank[b][:, :],
                                  ALU.add).then_inc(s, 1)

            def y_lo_copy(done):
                for n in range(2):
                    dve.wait_ge(y_hi_ready, 2 * done + n + 1)
                    dve.scalar_tensor_tensor(y_lo[:, 4 * n:4 * n + 4, :], bank[3 + n][:, :].rearrange("p (k c) -> p k c", k=4),
                                             slot_gate[:, 0:1], y_hi[:, 4 * n:4 * n + 4, :].bitcast(F32),
                                             ALU.mult, ALU.subtract).then_inc(y_lo_ready, 1)

            def add_scattered(done):
                for q in range(4):
                    dve.wait_ge(scattered, 4 * done + q + 1)
                    add_to_x(q // 2, q % 2, SCATTER_BANKS[q], added)

            def conv(l, steps):
                for s in steps:
                    tap, h = s // CH, s % CH
                    done = l * CH * TAPS + s
                    w = prm[:, l, Q_CONV_W + h * TAPS + tap:Q_CONV_W + h * TAPS + tap + 1]
                    src = uT[:, h, tap:tap + T]
                    if tap == 0:
                        if h == 0:
                            dve.wait_ge(conv_in, l + 1)
                        dve.tensor_scalar(cT[:, h, :], src, w, prm[:, l, Q_CONV_B + h:Q_CONV_B + h + 1],
                                          ALU.mult, ALU.add).then_inc(conv_step, 1)
                    else:
                        dve.wait_ge(conv_step, done - CH + 1)
                        dve.scalar_tensor_tensor(cT[:, h, :], src, w, cT[:, h, :], ALU.mult, ALU.add)\
                            .then_inc(conv_step, 1)

            norms = 0
            sums = 0
            for l in range(DEPTH):
                for i in range(3):
                    mixer_lo(l, i)
                sums += 2
                norm_rows(norms, sums)
                norms += 1
                turn_lo(3 * l, Q_ATTN_G, l)
                mixer_lo(l, 3)
                mixer_lo(l, 4)
                mixer_lo(l, 5)
                dve.wait_ge(blocks_used, layer_base(l) + 3)
                dve.wait_ge(gate_sig, l + 1)
                if l == 0:
                    dve.wait_ge(padded, 2)
                dve.tensor_tensor(uT[:, :, TAPS - 1:], bank[2][:, :].rearrange("p (h t) -> p h t", h=CH), sig[:, :, :],
                                  ALU.mult).then_inc(conv_in, 1)
                for i in range(6, 10):
                    mixer_lo(l, i)
                    conv(l, range(8 * (i - 6), 8 * (i - 5)))
                dve.wait_ge(blocks_used, layer_base(l) + 7)
                for b in range(2):
                    dve.tensor_copy(kT[:, 2 * b:2 * b + 2, :], bank[5 + b][:, :].rearrange("p (c t) -> p c t", c=2))\
                        .then_inc(k_in, 1)
                mixer_lo(l, 10)
                conv(l, range(32, 40))
                mixer_lo(l, 11)
                conv(l, range(40, 48))
                for h in range(HEADS + 1):
                    n = HEADS * l + h
                    if h < HEADS:
                        zb = bank[1 + h % 3]
                        dve.wait_ge(ln_ready, n + 1)
                        if n >= 2:
                            dve.wait_ge(c_ready, n - 1)
                        dve.scalar_tensor_tensor(sp_b[:, h % 2, :], zb[:, 0:Z], 0.0, lnb[:, h % 2, :], ALU.max, ALU.add)\
                            .then_inc(sp_raw, 1)
                        dve.wait_ge(sp_raw, n + 1)
                        dve.tensor_tensor(sp_b[:, h % 2, :], sp_b[:, h % 2, :], mask, ALU.mult).then_inc(sp_ready, 1)
                    if h >= 1:
                        dve.wait_ge(c_ready, n)
                        if n >= 3:
                            dve.wait_ge(pv_done, n - 2)
                        dve.scalar_tensor_tensor(wgt[:, (h - 1) % 2, :], bank[1 + (h - 1) % 3][:, 0:Z], 0.0, negm,
                                                 ALU.min, ALU.add).then_inc(arg_ready, 1)
                    if h < 7:
                        conv(l, range(48 + 2 * h, 50 + 2 * h))
                    if h == 1:
                        dve.wait_ge(pool_mixed, l + 1)
                        dve.tensor_copy(yT[:, :, :], bank[6][:, :].rearrange("p (g t) -> p g t", g=2)).then_inc(yT_ready, 1)
                dve.wait_ge(pool_done, l + 1)
                for odd in range(2):
                    rows = ob[:, :, :].rearrange("p t (g o c) -> p t g o c", g=2, o=2)[:, :, :, odd, :]
                    scale = prm[:, l, Q_POOL_S:Q_POOL_S + POOL].rearrange("p (g o c) -> p g o c", g=2, o=2)[:, :, odd, :]
                    ins = dve.tensor_tensor(rows, bank[7 - odd][:, 0:NT * P].rearrange("p (t g c) -> p t g c", t=NT, g=2),
                                            scale.unsqueeze(1).to_broadcast([P, NT, 2, HD]), ALU.mult)
                ins.then_inc(group_in, 1)
                dve.wait_ge(conv_turned, l + 1)
                link(dve.tensor_copy(cn[:, :, :], bank[0][:, :].rearrange("p (t c) -> p t c", t=NT)))
                link(dve.tensor_reduce(st[:, 56:58], cn[:, :, :], AX, ALU.add))
                link(dve.tensor_scalar(st[:, 58:60], st[:, 56:58], -1.0 / CONV, None, ALU.mult))
                for t in range(NT):
                    ins = dve.tensor_scalar(cn[:, t, :], cn[:, t, :], st[:, 58 + t:59 + t], None, ALU.add)
                ins.then_inc(group_in, 1)
                sums += 6
                dve.wait_ge(sumsq_done, sums)
                dve.tensor_scalar(st[:, 0:2], st[:, 54:56], 1.0 / CONV, LN_EPS, ALU.mult, ALU.add).then_inc(var_ready, 1)
                dve.wait_ge(var_ready, norms + 1)
                newton(norms, 2, 0)
                norms += 1
                for t in range(NT):
                    link(dve.scalar_tensor_tensor(cn[:, t, :], cn[:, t, :], st[:, 32 + t:33 + t],
                                                  prm[:, l, Q_LN_G:Q_LN_G + CONV], ALU.mult, ALU.mult))
                for t in range(NT):
                    ins = dve.tensor_tensor(cn[:, t, :], cn[:, t, :], prm[:, l, Q_LN_B:Q_LN_B + CONV], ALU.add)
                ins.then_inc(lin_ready, 1)
                sums += 2
                dve.wait_ge(sumsq_done, sums)
                link(dve.tensor_scalar(st[:, 0:2], st[:, 50:52], 1.0 / ATTN, RMS_EPS, ALU.mult, ALU.add))
                dve.tensor_scalar(st[:, 2:6], st[:, 52:56], 1.0 / CONV, RMS_EPS, ALU.mult, ALU.add).then_inc(var_ready, 1)
                dve.wait_ge(var_ready, norms + 1)
                newton(norms, 6, 0)
                norms += 1
                for t in range(NT):
                    dve.tensor_scalar(nat[:, t, 0:ATTN], bank[4 + t][:, :], st[:, 32 + t:33 + t], None, ALU.mult)
                    dve.tensor_scalar(nat[:, t, ATTN:ATTN + POOL], ob[:, t, :], st[:, 34 + t:35 + t], None, ALU.mult)
                    dve.tensor_scalar(nat[:, t, ATTN + POOL:D], cn[:, t, :], st[:, 36 + t:37 + t], None, ALU.mult)\
                        .then_inc(nat_ready, 1)
                turn_lo(3 * l + 1, Q_GN_G, l)
                mixer_lo(l, 12)
                if l == 0:
                    lo(Dense.base, HEAD_SLOTS[0], buf(Dense, 0))
                for n in range(2):
                    dve.wait_ge(blocks_used, layer_base(l) + W_IN_BLOCKS + 2 * n + 2)
                    for t in range(NT):
                        add_to_x(t, n, 4 + 2 * n + t, x_updated)
                    if l == 0 and n == 0:
                        lo(Dense.base + 1, HEAD_SLOTS[1], buf(Dense, 1))
                sums += 2
                if l == 1:
                    dve.wait_ge(moe_g_landed, 16)
                norm_rows(norms, sums, row_g[:, :] if l == 1 else None)
                norms += 1
                turn_lo(3 * l + 2, Q_FFN_G if l == 0 else None, l)
                if l == 0:
                    units(Dense)
                    dve.wait_ge(blocks_used, LAYER_BLOCKS)
                    for q in range(4):
                        add_to_x(q // 2, q % 2, Dense.acc[q], x_updated)

            dve.wait_ge(xn_hi_ready, 1)
            dve.tensor_tensor(xn_lo[:, :, :], nat[:, :, :], xn_hi[:, :, :].bitcast(F32), ALU.subtract).then_inc(xn_lo_ready, 1)
            dve.wait_ge(rw_hi_ready, 1)
            dve.tensor_tensor(rw_lo[:, :], rw32[:, :], rw_hi[:, :].bitcast(F32), ALU.subtract).then_inc(rw_lo_ready, 1)

            def tiles8(c):
                return rt[:, c:c + NT * E].rearrange("p (t e) -> p t e", t=NT)

            def per_tile(c):
                return rt[:, c:c + NT].unsqueeze(2).to_broadcast([P, NT, E])

            lg, top, gap, e2, g1 = 0, 16, R_GAP, R_EXP, 22
            g2, best, eq, sel1, sel2, lg2 = 24, 26, 32, 48, 64, 80
            msk, cmb, rank, cnt, over, cum = R_MASK, 112, 128, 144, 152, 160
            S, tmp, rankJ, maskJ, combJ, jf, top2 = 168, 200, 300, 324, R_GATES, 372, 380
            rev = cst[:, C_REV:C_REV + E].unsqueeze(1).to_broadcast([P, NT, E])
            dve.wait_ge(logits_ready, 1)
            link(dve.tensor_copy(tiles8(lg), bank[4][:, 0:NT * E].rearrange("p (t e) -> p t e", t=NT)))
            for src, m, sel in ((lg, top, sel1), (lg2, top2, sel2)):
                if src == lg2:
                    link(dve.scalar_tensor_tensor(tiles8(lg2), tiles8(sel1), LOWEST, tiles8(lg), ALU.mult, ALU.add))
                link(dve.tensor_reduce(rt[:, m:m + NT], tiles8(src), AX, ALU.max))
                link(dve.tensor_tensor(tiles8(eq), tiles8(src), per_tile(m), ALU.is_equal))
                link(dve.tensor_tensor(tiles8(eq), tiles8(eq), rev, ALU.mult))
                link(dve.tensor_reduce(rt[:, best:best + NT], tiles8(eq), AX, ALU.max))
                link(dve.tensor_tensor(tiles8(sel), rev, per_tile(best), ALU.is_equal))
            dve.tensor_tensor(rt[:, gap:gap + NT], rt[:, top2:top2 + NT], rt[:, top:top + NT], ALU.subtract)\
                .then_inc(gap_ready, 1)
            dve.tensor_tensor(tiles8(msk), tiles8(sel1), tiles8(sel2), ALU.add).then_inc(mask_ready, 1)
            dve.wait_ge(gap_exp, 1)
            link(dve.tensor_scalar(rt[:, g2:g2 + NT], rt[:, e2:e2 + NT], 1.0, None, ALU.add))
            link(dve.reciprocal(rt[:, g1:g1 + NT], rt[:, g2:g2 + NT]))
            link(dve.tensor_tensor(rt[:, g2:g2 + NT], rt[:, e2:e2 + NT], rt[:, g1:g1 + NT], ALU.mult))
            link(dve.tensor_tensor(tiles8(cmb), tiles8(sel1), per_tile(g1), ALU.mult))
            link(dve.tensor_tensor(tiles8(eq), tiles8(sel2), per_tile(g2), ALU.mult))
            link(dve.tensor_tensor(tiles8(cmb), tiles8(cmb), tiles8(eq), ALU.add))
            dve.wait_ge(rank_ready, 1)
            link(dve.tensor_copy(rt[:, rank:rank + 3 * E], bank[5][:, 0:3 * E]))
            link(dve.tensor_scalar(rt[:, over:over + E], rt[:, cnt:cnt + E], float(CAP), None, ALU.is_gt))
            pairs = rt[:, tmp:tmp + E * E].rearrange("p (a b) -> p a b", a=E)
            link(dve.tensor_tensor(pairs, cst[:, C_TRIE:C_TRIE + E * E].rearrange("p (a b) -> p a b", a=E),
                                   rt[:, over:over + E].unsqueeze(1).to_broadcast([P, E, E]), ALU.mult))
            link(dve.tensor_reduce(rt[:, cum:cum + E], pairs, AX, ALU.add))
            s3 = rt[:, S:S + EXTRA * E].rearrange("p (o e) -> p o e", o=EXTRA)
            link(dve.tensor_tensor(s3, cst[:, C_OIDX:C_OIDX + EXTRA * E].rearrange("p (o e) -> p o e", o=EXTRA),
                                   rt[:, cum:cum + E].unsqueeze(1).to_broadcast([P, EXTRA, E]), ALU.is_equal))
            link(dve.tensor_tensor(s3, s3, rt[:, over:over + E].unsqueeze(1).to_broadcast([P, EXTRA, E]), ALU.mult))
            for src, dst in ((rank, rankJ), (msk, maskJ), (cmb, combJ)):
                d = rt[:, dst:dst + NT * JOBCOLS].rearrange("p (t j) -> p t j", t=NT)
                link(dve.memset(rt[:, dst:dst + NT * JOBCOLS], 0.0))
                link(dve.tensor_copy(d[:, :, 0:E], tiles8(src)))
                for t in range(NT):
                    m3 = rt[:, tmp:tmp + EXTRA * E].rearrange("p (o e) -> p o e", o=EXTRA)
                    link(dve.tensor_tensor(m3, s3, rt[:, src + t * E:src + (t + 1) * E].unsqueeze(1)
                                           .to_broadcast([P, EXTRA, E]), ALU.mult))
                    link(dve.tensor_reduce(d[:, t, E:E + EXTRA], m3, AX, ALU.add))
                if src == rank:
                    link(dve.tensor_scalar(d[:, :, E:E + EXTRA], d[:, :, E:E + EXTRA], -float(CAP), None, ALU.add))
            m3 = rt[:, tmp:tmp + EXTRA * E].rearrange("p (o e) -> p o e", o=EXTRA)
            link(dve.tensor_tensor(m3, s3, cst[:, C_EIDX:C_EIDX + E].unsqueeze(1).to_broadcast([P, EXTRA, E]), ALU.mult))
            link(dve.tensor_reduce(rt[:, jf + 1:jf + 1 + EXTRA], m3, AX, ALU.add))
            link(dve.tensor_reduce(rt[:, jf:jf + 1], rt[:, over:over + E], AX, ALU.add))
            link(dve.tensor_scalar(rt[:, jf:jf + 1], rt[:, jf:jf + 1], float(E), None, ALU.add))
            link(dve.memset(slot_gate[:, :], 0.0))
            dve.tensor_scalar(hotT[:, :], cst[:, C_POOL:C_POOL + T], 0.0, None, ALU.mult).then_inc(hotT_ready, 1)
            dve.tensor_copy(jobs[:, :], rt[:, jf:jf + 1 + EXTRA]).then_inc(route_ready, 1)

            def one_hot(j):
                for t in range(NT):
                    dve.tensor_scalar(hot[:, t, :], cst[:, C_IOTA:C_IOTA + CAP],
                                      rt[:, bass.ds(rankJ + t * JOBCOLS + j, 1)],
                                      rt[:, bass.ds(maskJ + t * JOBCOLS + j, 1)],
                                      ALU.is_equal, ALU.mult).then_inc(hot_ready, 1)

            one_hot(0)
            dve.wait_ge(route_ready, 1)
            njobs = dve.value_load(jobs[0:1, 0:1], min_val=E, max_val=E + EXTRA)
            with dve.Fori(0, njobs) as j:
                part = job_part(j)
                lo(part.base, HEAD_SLOTS[0], buf(part, 0))
                for b in range(2):
                    dve.wait_ge(xe_hi_ready, 2 * j + b + 1)
                    dve.tensor_tensor(xeT_lo[:, 4 * b:4 * b + 4, :], bank[5 + b][:, :].rearrange("p (k c) -> p k c", k=4),
                                      xeT_hi[:, 4 * b:4 * b + 4, :].bitcast(F32), ALU.subtract).then_inc(xe_lo_ready, 1)
                lo(part.base + 1, HEAD_SLOTS[1], buf(part, 1))

                def add_and_keep_hot():
                    add_scattered(j)
                    dve.wait_ge(hot_turned, j + 1)
                    dve.tensor_copy(hotT[:, :], bank[7][:, 0:T])
                    dve.tensor_copy(slot_gate[:, :], bank[7][:, T:T + 1]).then_inc(hotT_ready, 1)

                units(part, lambda: y_lo_copy(j), add_and_keep_hot, lambda: one_hot(j + 1))
            y_lo_copy(njobs)
            add_scattered(njobs)
            sums += 2
            dve.wait_ge(sumsq_done, sums)
            dve.tensor_scalar(st[:, 0:2], st[:, 48:50], 1.0 / D, RMS_EPS, ALU.mult, ALU.add).then_inc(var_ready, 1)
            dve.wait_ge(var_ready, norms + 1)
            newton(norms, 2, 0)
            dve.wait_ge(final_g_landed, 16)
            for t in range(NT):
                dve.scalar_tensor_tensor(nat[:, t, :], xs[:, t, :], st[:, 32 + t:33 + t], row_g[:, :], ALU.mult, ALU.mult)\
                    .then_inc(out_done, 1)

        @block.tensor
        def _(pe):
            def three(out_ap, l_hi, l_lo, r_hi, r_lo, start, stop, **kw):
                pe.matmul(out_ap, l_hi, r_hi, start=start, stop=False, **kw)
                pe.matmul(out_ap, l_hi, r_lo, start=False, stop=False, **kw)
                return pe.matmul(out_ap, l_lo, r_hi, start=False, stop=stop, **kw)

            def turn(e):
                pe.wait_ge(nat_ready, 2 * e + 2)
                for b in range(4):
                    for k in (2 * b, 2 * b + 1):
                        for t in range(NT):
                            c = (k % 2) * T + t * P
                            ins = pe.transpose(bank[turn_banks(e)[b]][:, c:c + P], nat[:, t, k * P:(k + 1) * P], ident)
                    ins.then_inc(turned, 1)

            def mixer_block(l, i):
                n = layer_base(l) + i
                pe.wait_ge(split_lo, n + 1)
                return whi[:, n % 3, :], wlo[:, n % 3, :]

            def rows_out(l, i, half, banks):
                wh, wl = mixer_block(l, i)
                for t in range(NT):
                    for k in range(4):
                        kk = 4 * half + k
                        ins = three(bank[banks[t]][:, :], xT_hi[:, kk, t * P:(t + 1) * P], xT_lo[:, kk, t * P:(t + 1) * P],
                                    wh[:, k * 512:(k + 1) * 512], wl[:, k * 512:(k + 1) * 512], kk == 0, kk == KD - 1)
                ins.then_inc(blocks_used, 1)

            def cols_out(l, i, k0, nk, width, first, outs):
                wh, wl = mixer_block(l, i)
                for c, o in enumerate(outs):
                    for k in range(nk):
                        a = k * width + first + c * P
                        kk = k0 + k
                        ins = three(o, wh[:, a:a + P], wl[:, a:a + P], xT_hi[:, kk, :], xT_lo[:, kk, :],
                                    kk == 0 and c % 2 == 0, kk == KD - 1, skip_group_check=True)
                return ins

            def halves(b):
                return [bank[b][:, 0:T], bank[b][:, T:2 * T]]

            def gate_up(part, pos, b, half, banks):
                pe.wait_ge(split_lo, part.base + pos + 1)
                for t in range(part.tiles):
                    for k in range(4):
                        kk = 4 * half + k
                        ins = three(bank[banks[t]][:, :], xT_hi[:, kk, t * P:(t + 1) * P], xT_lo[:, kk, t * P:(t + 1) * P],
                                    whi[:, b, k * 512:(k + 1) * 512], wlo[:, b, k * 512:(k + 1) * 512],
                                    kk == 0, kk == KD - 1)
                ins.then_inc(blocks_used, 1)

            def turn_h(part, i):
                w = part.tiles * P
                pe.wait_ge(h_ready, part.gu0 + part.tiles * (i + 1))
                for f in range(2):
                    for t in range(part.tiles):
                        ins = pe.transpose(bank[2][:, f * w + t * P:f * w + (t + 1) * P], hn[:, t, f * P:(f + 1) * P], ident)
                ins.then_inc(h_turned, 1)

            def down(part, pos, b, i, last):
                pe.wait_ge(split_lo, part.base + pos + 1)
                pe.wait_ge(hT_lo_ready, part.unit0 + i + 1)
                for t in range(part.tiles):
                    for f in range(2):
                        for n in range(2):
                            c = f * D + n * 512
                            ins = three(bank[part.acc[2 * t + n]][:, :], hT_hi[:, f, t * P:(t + 1) * P],
                                        hT_lo[:, f, t * P:(t + 1) * P], whi[:, b, c:c + 512], wlo[:, b, c:c + 512],
                                        False, last and f == 1, skip_group_check=True)
                ins.then_inc(blocks_used, 1)

            def prime(part):
                for b in part.acc:
                    pe.matmul(bank[b][:, :].rearrange("p (a c) -> p a c", a=4), zeros[:, :], zeros[:, :].unsqueeze(1).to_broadcast([P, 4, P]), start=True, stop=False, skip_group_check=True)

            def unit(part, i, u, after_a=None, after_b=None):
                pos = 3 * i - 1
                if part.tiles == NT:
                    pe.wait_ge(h_ready, part.gu0 + part.tiles * i)
                elif not after_a:
                    pe.wait_ge(added, 4 * part.parts)
                gate_up(part, pos, buf(part, 2), 0, gu_banks(part, 1 - u))
                if after_a:
                    after_a()
                turn_h(part, i - 1)
                gate_up(part, pos + 1, buf(part, 3), 1, gu_banks(part, 1 - u))
                if after_b:
                    after_b()
                down(part, pos + 2, buf(part, 4), i - 1, False)

            def ffn(part, after_a1=None, after_b1=None, tail_extra=None):
                gate_up(part, 0, buf(part, 0), 0, gu_banks(part, 0))
                gate_up(part, 1, buf(part, 1), 1, gu_banks(part, 0))
                if not after_a1:
                    prime(part)
                unit(part, 1, 0, after_a1, after_b1)
                with pe.Fori(0, PAIRS) as k:
                    for u in (1, 0):
                        unit(part, 2 * k + 3 - u, u)
                unit(part, UNITS - 1, 1)
                turn_h(part, UNITS - 1)
                if tail_extra:
                    tail_extra()
                down(part, FFN_BLOCKS - 1, buf(part, FFN_BLOCKS - 1), UNITS - 1, True)

            for l in range(DEPTH):
                if l == 0:
                    pe.wait_ge(c_landed, 16)
                    pe.wait_ge(padded, 2)
                turn(3 * l)
                pe.wait_ge(xT_lo_ready, 8 * (3 * l + 1))
                cols_out(l, 0, 0, KD, CONV, 0, halves(0)).then_inc(blocks_used, 1)
                for half in range(2):
                    wh, wl = mixer_block(l, 1 + half)
                    for t in range(NT):
                        for k in range(4):
                            kk = 4 * half + k
                            three(halves(1)[t], xT_hi[:, kk, t * P:(t + 1) * P], xT_lo[:, kk, t * P:(t + 1) * P],
                                  wh[:, k * 512:k * 512 + POOL], wl[:, k * 512:k * 512 + POOL],
                                  kk == 0 and t == 0, kk == KD - 1, skip_group_check=True)
                    cols_out(l, 1 + half, 4 * half, 4, 512, POOL, halves(2)).then_inc(blocks_used, 1)
                for q, banks in ((0, (3, 4)), (1, (5, 6))):
                    for half in range(2):
                        cols_out(l, 3 + 2 * q + half, 4 * half, 4, 512, 0, halves(banks[0]) + halves(banks[1]))\
                            .then_inc(blocks_used, 1)
                pe.wait_ge(gate_sig, l + 1)
                for half in range(2):
                    rows_out(l, 7 + half, half, (0, 7))

                pe.wait_ge(q_in, 2 * l + 2)
                pe.wait_ge(k_in, 2 * l + 2)
                pe.wait_ge(conv_in, l + 1)
                pe.wait_ge(pool_in, l + 1)
                for s in range(HEADS + 2):
                    if s < HEADS:
                        n = HEADS * l + s
                        zb = bank[1 + s % 3]
                        if s >= 3:
                            pe.wait_ge(arg_ready, n - 2)
                        r = slice((s % 2) * HD, (s % 2 + 1) * HD)
                        pe.matmul(zb[:, 0:T], kT[r, s // 2, 0:P], qT[r, s // 2, :], start=True, stop=False,
                                  skip_group_check=True)
                        pe.matmul(zb[:, T:Z], kT[r, s // 2, P:T], qT[r, s // 2, P:T], start=False, stop=True,
                                  skip_group_check=True).then_inc(z_ready, 1)
                    if s == 0:
                        for g in range(len(WINDOWS)):
                            o = bank[6][(g % 2) * HD:(g % 2 + 1) * HD, (g // 2) * T:(g // 2 + 1) * T]
                            b0 = C_POOL + g * Z
                            pe.matmul(o, up_n[:, 0, g * HD:(g + 1) * HD], cst[:, b0:b0 + T], start=True, stop=False,
                                      skip_group_check=True)
                            ins = pe.matmul(o[:, P:T], up_n[:, 1, g * HD:(g + 1) * HD], cst[:, b0 + T:b0 + Z], start=False,
                                            stop=True, skip_group_check=True)
                        ins.then_inc(pool_mixed, 1)
                    if 1 <= s <= HEADS:
                        n = HEADS * l + s - 1
                        zb, sp_h = bank[1 + (s - 1) % 3], sp_b[:, (s - 1) % 2, :]
                        pe.wait_ge(sp_ready, n + 1)
                        pe.matmul(zb[:, 0:T], cst[:, C_TRIN:C_TRIN + P], sp_h[:, 0:T], start=False, stop=False,
                                  skip_group_check=True)
                        pe.matmul(zb[:, P:T], cst[:, C_ONEN:C_ONEN + P], sp_h[:, T:Z], start=False, stop=False,
                                  skip_group_check=True)
                        pe.matmul(zb[:, T:Z], cst[:, C_TRIN:C_TRIN + P], sp_h[:, T:Z], start=False, stop=True,
                                  skip_group_check=True).then_inc(c_ready, 1)
                    if s == 3:
                        pe.wait_ge(yT_ready, l + 1)
                        pe.wait_ge(v_in, 2 * l + 2)
                        for t in range(NT):
                            for g in range(len(WINDOWS)):
                                r = slice((g % 2) * HD, (g % 2 + 1) * HD)
                                c = Q_POOL_W + (g // 2) * HD
                                o = t * P + (g // 2) * HD
                                ins = pe.matmul(bank[7 - g % 2][:, o:o + HD],
                                                yT[r, g // 2, t * P:(t + 1) * P], prm[r, l, c:c + HD], start=True, stop=True)
                        ins.then_inc(pool_done, 1)
                    if s >= 2:
                        n, h = HEADS * l + s - 2, s - 2
                        w = wgt[:, h % 2, :]
                        v0, v1 = (vn[:, t, h * HD:(h + 1) * HD] for t in range(NT))
                        if h == 0:
                            pe.wait_ge(v_in, 2 * l + 2)
                        pe.wait_ge(w_ready, n + 1)
                        pe.matmul(bank[4][:, h * HD:(h + 1) * HD], w[:, 0:P], v0, start=True, stop=True)
                        pe.matmul(bank[5][:, h * HD:(h + 1) * HD], w[:, P:T], v0, start=True, stop=False)
                        pe.matmul(bank[5][:, h * HD:(h + 1) * HD], w[:, T:Z], v1, start=False, stop=True).then_inc(pv_done, 1)
                pe.wait_ge(conv_step, CH * TAPS * (l + 1))
                for t in range(NT):
                    for h in range(CH):
                        ins = pe.transpose(bank[0][:, t * CONV + h * P:t * CONV + (h + 1) * P], cT[:, h, t * P:(t + 1) * P], ident)
                ins.then_inc(conv_turned, 1)
                turn(3 * l + 1)
                pe.wait_ge(xT_lo_ready, 8 * (3 * l + 2))
                for n in range(2):
                    for half in range(2):
                        rows_out(l, W_IN_BLOCKS + 2 * n + half, half, (4 + 2 * n, 5 + 2 * n))
                turn(3 * l + 2)
                pe.wait_ge(xT_lo_ready, 8 * (3 * l + 3))
                if l == 0:
                    ffn(Dense)

            pe.wait_ge(rw_lo_ready, 1)
            for t in range(NT):
                for k in range(KD):
                    a, c = xT_hi[:, k, t * P:(t + 1) * P], xT_lo[:, k, t * P:(t + 1) * P]
                    rh, rl = rw_hi[:, k * E:(k + 1) * E], rw_lo[:, k * E:(k + 1) * E]
                    o = bank[4][:, t * E:(t + 1) * E]
                    three(o, a, c, rh, rl, k == 0, False)
                    ins = pe.matmul(o, c, rl, start=False, stop=k == KD - 1)
            ins.then_inc(logits_ready, 1)
            pe.wait_ge(mask_ready, 1)
            m = [rt[:, R_MASK + t * E:R_MASK + (t + 1) * E] for t in range(NT)]
            before, ones = cst[:, C_RANK:C_RANK + P], cst[:, C_ONE:C_ONE + P]
            o = [bank[5][:, c * E:(c + 1) * E] for c in range(3)]
            pe.matmul(o[0], before, m[0], start=True, stop=True)
            pe.matmul(o[1], ones, m[0], start=True, stop=False)
            pe.matmul(o[1], before, m[1], start=False, stop=True)
            pe.matmul(o[2], ones, m[0], start=True, stop=False)
            pe.matmul(o[2], ones, m[1], start=False, stop=True).then_inc(rank_ready, 1)

            def gather(j):
                pe.wait_ge(hot_ready, 2 * j + 2)
                for b in range(2):
                    for k in range(4 * b, 4 * b + 4):
                        o = bank[5 + b][:, (k % 4) * CAP:(k % 4 + 1) * CAP]
                        for t in range(NT):
                            pe.matmul(o, xn_hi[:, t, k * P:(k + 1) * P], hot[:, t, :], start=t == 0, stop=False)
                            ins = pe.matmul(o, xn_lo[:, t, k * P:(k + 1) * P], hot[:, t, :], start=False, stop=t == NT - 1)
                    ins.then_inc(gathered, 1)

            def scatter(done, with_unit0=True):
                pe.wait_ge(y_lo_ready, 2 * done + 2)
                for q in range(4):
                    t, n = q // 2, q % 2
                    if q == 3 and with_unit0:
                        pe.wait_ge(h_ready, job_part(done).gu0 + 1)
                    o = bank[SCATTER_BANKS[q]][:, :].rearrange("p (k c) -> p k c", k=4)
                    pe.matmul(o, hotT[:, t * P:(t + 1) * P], y_hi[:, 4 * n:4 * n + 4, :], start=True, stop=False)
                    pe.matmul(o, hotT[:, t * P:(t + 1) * P], y_lo[:, 4 * n:4 * n + 4, :], start=False, stop=True)\
                        .then_inc(scattered, 1)

            pe.wait_ge(xn_lo_ready, 1)
            gather(0)
            pe.wait_ge(route_ready, 1)
            njobs = pe.value_load(jobs[0:1, 0:1], min_val=E, max_val=E + EXTRA)
            with pe.Fori(0, njobs) as j:
                part = job_part(j)

                def scatter_and_prime():
                    scatter(j)
                    prime(part)

                def turn_hot():
                    pe.wait_ge(added, 4 * j + 1)
                    for t in range(NT):
                        pe.transpose(bank[7][:, t * P:(t + 1) * P], hot[:, t, :].bitcast(F32), ident)
                    for t in range(NT):
                        ins = pe.matmul(bank[7][:, T:T + 1], hot[:, t, :].bitcast(F32),
                                        rt[:, bass.ds(R_GATES + t * JOBCOLS + j, 1)], start=t == 0, stop=t == NT - 1,
                                        skip_group_check=True)
                    ins.then_inc(hot_turned, 1)

                pe.wait_ge(xe_lo_ready, 2 * j + 2)
                ffn(part, scatter_and_prime, turn_hot, lambda: gather(j + 1))
            scatter(njobs, False)


SCATTER_BANKS = (7, 5, 6, 0)


def gate_up_pos(i):
    return 3 * i + (i < 1)


def turn_banks(e):
    return (4, 5, 6, 7) if e % 3 == 0 else (0, 1, 2, 3)


def gu_bank(part, t, u):
    return t if part.tiles == NT else u


def gu_banks(part, u):
    return [gu_bank(part, t, u) for t in range(part.tiles)]


def _columns(v):
    return v.reshape(-1, P).T


def _params(inp):
    rows = []
    for l in range(DEPTH):
        cw = inp["conv_w"][l].reshape(TAPS, CH, P).transpose(2, 1, 0).reshape(P, CH * TAPS)
        pw = inp["pool_w"][l].reshape(2, 2, HD, HD).transpose(1, 2, 0, 3).reshape(P, 2 * HD)
        wide = [np.broadcast_to(inp[k][l][None, :], (P, inp[k].shape[1])) for k in ("pool_scale", "conv_ln_g", "conv_ln_b")]
        rows.append(np.concatenate([_columns(inp["attn_norm_g"][l]), _columns(inp["ffn_norm_g"][l]),
                                    _columns(inp["group_norm_g"][l]), cw, _columns(inp["conv_b"][l]), pw, *wide], axis=1))
    return np.ascontiguousarray(np.stack(rows, axis=1))


def kernel(**inputs):
    import concourse.bacc as bacc
    from concourse.bass_utils import run_bass_kernel_spmd

    inp = {k: np.asarray(v) for k, v in inputs.items()}
    arrays = {
        "x": inp["x"], "w_in": inp["w_in"], "w_out": inp["w_out"],
        "dense_gate": inp["dense_w_gate"], "dense_up": inp["dense_w_up"], "dense_down": inp["dense_w_down"],
        "moe_gate": inp["moe_w_gate"], "moe_up": inp["moe_w_up"], "moe_down": inp["moe_w_down"],
        "params": _params(inp),
        "router": np.ascontiguousarray(inp["router_w"][0].reshape(KD, P, E).transpose(1, 0, 2).reshape(P, KD * E)),
        "moe_g": np.ascontiguousarray(np.broadcast_to(inp["ffn_norm_g"][1][None, :], (P, D))),
        "final_g": np.ascontiguousarray(np.broadcast_to(inp["final_norm_g"][None, :], (P, D))),
        "consts": constants(),
    }
    arrays = {f"in_{k}": np.ascontiguousarray(a) for k, a in arrays.items()}
    nc = bacc.Bacc("TRN2", target_bir_lowering=False, num_devices=1)
    args = [nc.dram_tensor(k, a.shape, mybir.dt.from_np(a.dtype), kind="ExternalInput").ap() for k, a in arrays.items()]
    out = nc.dram_tensor("out", inp["x"].shape, F32, kind="ExternalOutput").ap()
    build(nc, *args, out)
    r = run_bass_kernel_spmd(nc, [arrays], core_ids=[0])
    return r.results[0]["out"]
```

```python
from contextlib import ExitStack

import numpy as np

import concourse.bass as bass
from concourse import mybir

ALU = mybir.AluOpType
ACT = mybir.ActivationFunctionType
AX = mybir.AxisListType.X
F32 = mybir.dt.float32
F32R = mybir.dt.float32r
BF16 = mybir.dt.bfloat16
I32 = mybir.dt.int32

P = 128
DEPTH = 2
T = 256
NT = T // P
D = 1024
KD = D // P
ATTN = 512
HEADS = 8
HD = 64
POOL = 256
WINDOWS = (2, 4, 8, 16)
CONV = 256
CH = CONV // P
TAPS = 31
IN_COLS = 3 * ATTN + POOL + 2 * CONV
F = 2816
UF = 256
UNITS = F // UF
E = 8
CAP = 128
EXTRA = 3
JOBCOLS = E + EXTRA + 1
RMS_EPS = 1e-6
LN_EPS = 1e-5
BIG = 2.0 ** 100
LOWEST = -3e38
Z = T + P

W_IN_BLOCKS = 9
W_OUT_BLOCKS = 4
MIX_BLOCKS = W_IN_BLOCKS + W_OUT_BLOCKS
FFN_BLOCKS = 3 * UNITS
LAYER_BLOCKS = MIX_BLOCKS + FFN_BLOCKS
RAW = 9
AHEAD = 6
HEAD_SLOTS = (6, 7)
TAIL_SLOT = 8
PAIRS = (UNITS - 3) // 2
LOADS = (UNITS - 1) // 2
FILL = 32

PROJ = [(0, 8, 3 * ATTN + POOL + CONV, CONV)]
for first in (3 * ATTN, 0, ATTN, 2 * ATTN):
    PROJ += [(0, 4, first, 512), (4, 4, first, 512)]

C_ID = 0
C_NEG = C_ID + P
C_TRIN = C_NEG + Z
C_ONEN = C_TRIN + P
C_CENTRE = C_ONEN + P
C_POOL = C_CENTRE + 3 * P
C_RANK = C_POOL + len(WINDOWS) * Z
C_ONE = C_RANK + P
C_IOTA = C_ONE + P
C_REV = C_IOTA + P
C_TRIE = C_REV + E
C_OIDX = C_TRIE + E * E
C_EIDX = C_OIDX + EXTRA * E
C_FOLD = C_EIDX + E
C_ONECOL = C_FOLD + E
C_COLS = C_ONECOL + 1

J_RANK, J_MASK, J_GATE, J_EXPERT, J_ROWS = 0, NT, 2 * NT, 3 * NT, 3 * NT + 1
R_GAP, R_EXP, R_OTHER = J_ROWS * JOBCOLS, J_ROWS * JOBCOLS + NT, J_ROWS * JOBCOLS + 2 * NT
R_COLS = 448

Q_ATTN_G, Q_FFN_G, Q_GN_G = 0, KD, 2 * KD
Q_CONV_W = 3 * KD
Q_CONV_B = Q_CONV_W + CH * TAPS
Q_POOL_W = Q_CONV_B + CH
Q_POOL_S = Q_POOL_W + 2 * HD
Q_LN_G = Q_POOL_S + POOL
Q_LN_B = Q_LN_G + CONV
Q_COLS = Q_LN_B + CONV


POOL_TAPS = 14
DVE_TAPS = TAPS - POOL_TAPS
DVE_STEPS = CH * DVE_TAPS


def constants():
    c = np.zeros((P, C_COLS), np.float32)
    p = np.arange(P)[:, None]
    col = np.arange(P)[None, :]
    c[:, C_ID:C_ID + P] = p == col
    t = np.concatenate([np.arange(T), np.arange(P, T)])[None, :]
    s = np.concatenate([np.zeros(T), np.full(P, P)])[None, :] + p
    c[:, C_NEG:C_NEG + Z] = np.where(s < t, 0.0, -BIG)
    c[:, C_TRIN:C_TRIN + P] = np.where(p >= col, -1.0, 0.0)
    c[:, C_ONEN:C_ONEN + P] = -1.0
    c[:, C_CENTRE:C_CENTRE + 3 * P] = -1.0 / CONV
    c[:, C_CENTRE + P:C_CENTRE + 2 * P] += p == col
    for g, w in enumerate(WINDOWS):
        count = np.minimum(t + 1, w)
        c[:, C_POOL + g * Z:C_POOL + (g + 1) * Z] = np.where((s <= t) & (s > t - w), 1.0 / count, 0.0) - (s == t)
    c[:, C_RANK:C_RANK + P] = p < col
    c[:, C_ONE:C_ONE + P] = 1.0
    c[:, C_IOTA:C_IOTA + P] = col
    c[:, C_REV:C_REV + E] = E - np.arange(E)
    c[:, C_TRIE:C_TRIE + E * E] = (np.arange(E)[None, :] < np.arange(E)[:, None]).reshape(1, -1)
    c[:, C_OIDX:C_OIDX + EXTRA * E] = np.repeat(np.arange(EXTRA), E)[None, :]
    c[:, C_EIDX:C_EIDX + E] = np.arange(E)
    c[:, C_FOLD:C_FOLD + E] = (p % E == np.arange(E)[None, :]) & (p < 2 * E)
    c[:, C_ONECOL] = 1.0
    return c


def raw_slot(i):
    return HEAD_SLOTS[0] if i == 0 else (i - 1) % 6


def build(nc, x, w_in, w_out, dense_gate, dense_up, dense_down, moe_gate, moe_up, moe_down, params, router, moe_g,
          final_g, consts, out):
    with ExitStack() as ctx:
        def sb(name, shape, dt=F32):
            return ctx.enter_context(nc.sbuf_tensor(name, shape, dt))

        def sem(name):
            return ctx.enter_context(nc.semaphore(name))

        cst = sb("cst", [P, C_COLS])
        prm = sb("prm", [P, DEPTH, Q_COLS])
        rw32 = sb("rw32", [P, KD * E])
        raw = sb("raw", [P, RAW, 2048])
        whi = sb("whi", [P, 3, 2048], F32R)
        wlo = sb("wlo", [P, 3, 2048], F32R)
        xs = sb("xs", [P, NT, D])
        nat = sb("nat", [P, NT, D])
        xT_hi = sb("xT_hi", [P, KD, T], F32R)
        xT_lo = sb("xT_lo", [P, KD, T], F32R)
        hid = sb("hid", [P, 2, NT, UF])
        hs, hn = hid[:, 0], hid[:, 1]
        junk = hid[:, :, :, :].rearrange("p a t c -> p (a t c)")
        hT_hi = sb("hT_hi", [P, 2, T], F32R)
        hT_lo = sb("hT_lo", [P, 2, T], F32R)
        zeros = sb("zeros", [P, P], BF16)
        id_b = sb("id_b", [P, P], BF16)
        neg_b = sb("neg_b", [P, Z], BF16)
        st = sb("st", [P, 64])
        jobs = sb("jobs", [P, 1 + EXTRA], I32)

        with ExitStack() as mixers:
            def mixer_sb(name, shape):
                return mixers.enter_context(nc.sbuf_tensor(name, shape, F32))

            qT = mixer_sb("qT", [P, ATTN // P, T])
            kT = mixer_sb("kT", [P, ATTN // P, T])
            vn = mixer_sb("vn", [P, NT, ATTN])
            wgt = mixer_sb("wgt", [P, 2, Z])
            up_n = mixer_sb("up_n", [P, NT, POOL])
            sig = mixer_sb("sig", [P, CH, T])
            uT = mixer_sb("uT", [P, CH, TAPS - 1 + T])
            cT = mixer_sb("cT", [P, CH, T])
            cn = mixer_sb("cn", [P, NT, CONV])
        ob = sig
        flat = nat[:, :, :].rearrange("p t d -> p (t d)")
        lnb = flat[:, 0:2 * Z].rearrange("p (b z) -> p b z", b=2)
        sp_b = flat[:, 2 * Z:4 * Z].rearrange("p (b z) -> p b z", b=2)
        yT = flat[:, 4 * Z:4 * Z + 2 * T].rearrange("p (g t) -> p g t", g=2)

        xn_hi = sb("xn_hi", [P, NT, D], F32R)
        xn_lo = sb("xn_lo", [P, NT, D], F32R)
        rw = sb("rw", [P, KD, 2, E], F32R)
        hot = sb("hot", [P, NT, CAP], F32R)
        hotT = sb("hotT", [P, T], F32R)
        slot_gate = sb("slot_gate", [P, 1])
        rt = sb("rt", [P, R_COLS])
        row_g = sb("row_g", [P, D])
        bank = [ctx.enter_context(nc.psum_tensor(f"bank{b}", [P, 512], F32)) for b in range(8)]

        ident = cst[:, C_ID:C_ID + P]
        logitsT = junk[0:2 * E, 0:T]
        cP = cn
        tapped = junk[:, 2 * CONV:4 * CONV].rearrange("p (h t) -> p h t", h=CH)
        xeT_hi, xeT_lo = xT_hi[:, :, 0:CAP], xT_lo[:, :, 0:CAP]
        y_hi, y_lo = xT_hi[:, :, CAP:T], xT_lo[:, :, CAP:T]

        x_landed, ident_landed, gains_landed, c_landed = (sem(n) for n in ("x_landed", "ident_landed", "gains_landed", "c_landed"))
        p_landed = [sem(f"p_landed{l}") for l in range(DEPTH)]
        moe_g_landed, final_g_landed = sem("moe_g_landed"), sem("final_g_landed")
        slot_landed = [sem(f"slot_landed{s}") for s in range(RAW)]
        split_hi, split_lo, blocks_used = sem("split_hi"), sem("split_lo"), sem("blocks_used")
        sumsq_done = sem("sumsq_done")
        var_ready, ln_done, rsqrt_rough = sem("var_ready"), sem("ln_done"), sem("rsqrt_rough")
        nat_ready, turned, xT_hi_ready, xT_lo_ready = sem("nat_ready"), sem("turned"), sem("xT_hi_ready"), sem("xT_lo_ready")
        gate_sig, conv_in, pool_in, q_in, k_in, v_in = (sem(n) for n in ("gate_sig", "conv_in", "pool_in", "q_in", "k_in", "v_in"))
        z_ready, abs_done, exp_done, ln_ready = sem("z_ready"), sem("abs_done"), sem("exp_done"), sem("ln_ready")
        sp_ready, c_ready, w_ready, pv_done = (sem(n) for n in ("sp_ready", "c_ready", "w_ready", "pv_done"))
        pool_mixed, yT_ready, pool_done = sem("pool_mixed"), sem("yT_ready"), sem("pool_done")
        padded, conv_step, conv_turned = sem("padded"), sem("conv_step"), sem("conv_turned")
        pool_step, conv_joined, attn_nat_ready = sem("pool_step"), sem("conv_joined"), sem("attn_nat_ready")
        pool_out, lin_ready, swish_done = (sem(n) for n in ("pool_out", "lin_ready", "swish_done"))
        table_ready = sem("table_ready")
        x_updated, silu_ready, h_ready = sem("x_updated"), sem("silu_ready"), sem("h_ready")
        h_turned, hT_hi_ready, hT_lo_ready = sem("h_turned"), sem("hT_hi_ready"), sem("hT_lo_ready")
        xn_hi_ready, xn_lo_ready, rw_hi_ready, rw_lo_ready = (sem(n) for n in ("xn_hi_ready", "xn_lo_ready", "rw_hi_ready", "rw_lo_ready"))
        logitsT_ready, logitsT_copied = sem("logitsT_ready"), sem("logitsT_copied")
        biases_ready = sem("biases_ready")
        logits_ready, gap_ready, gap_exp, mask_ready, rank_ready = (
            sem(n) for n in ("logits_ready", "gap_ready", "gap_exp", "mask_ready", "rank_ready"))
        njobs_ready = sem("njobs_ready")
        route_ready, hot_ready, gathered, xe_hi_ready, xe_lo_ready = (
            sem(n) for n in ("route_ready", "hot_ready", "gathered", "xe_hi_ready", "xe_lo_ready"))
        y_hi_ready, y_lo_ready, scattered, added = sem("y_hi_ready"), sem("y_lo_ready"), sem("scattered"), sem("added")
        hot_turned, hotT_ready = sem("hot_turned"), sem("hotT_ready")
        dve_step, out_done, out_landed = sem("dve_step"), sem("out_done"), sem("out_landed")

        def layer_base(l):
            return l * LAYER_BLOCKS

        class Dense:
            tiles = NT
            base = MIX_BLOCKS
            unit0 = 0
            gu0 = 0
            parts = 0
            loop_fills, head_fills, tail_fills = 2, 1, 0
            acc = (3, 4, 5, 6)

        def job_part(j):
            class Job:
                tiles = 1
                base = layer_base(1) + MIX_BLOCKS + FFN_BLOCKS * j
                unit0 = UNITS + UNITS * j
                gu0 = NT * UNITS + UNITS * j
                parts = 1 + j
                loop_fills, head_fills, tail_fills = 4 + LOADS + LOADS * j, 3 + j, 1 + j
                acc = (3, 4)
            return Job

        def buf(part, pos):
            return ((MIX_BLOCKS if part.tiles == NT else layer_base(1) + MIX_BLOCKS) + pos) % 3

        def mixer_fill(l, i):
            if i == 0:
                return 1 if l == 0 else 3
            return (0 if l == 0 else 2 + LOADS) + (i - 1) // 6 + 1

        block = ctx.enter_context(nc.Block())

        @block.sync
        def _(sp):
            def load(n, slot, pieces):
                if not (isinstance(n, int) and n < AHEAD):
                    sp.wait_ge(split_lo, n - AHEAD + 1)
                for dst, src in pieces:
                    sp.dma_start(dst, src).then_inc(slot_landed[slot], 16)

            def rows(w, k0, nk, c0, ncols):
                return w[k0 * P:(k0 + nk) * P, c0:c0 + ncols].rearrange("(k p) c -> p k c", p=P)

            def mixer_block(l, i):
                w, (k0, nk, c0, ncols) = (w_in[l], PROJ[i]) if i < W_IN_BLOCKS else (
                    w_out[l], (4 * ((i - W_IN_BLOCKS) // 2), 4, 512 * ((i - W_IN_BLOCKS) % 2), 512))
                s = raw_slot(i)
                dst = raw[:, s, :].rearrange("p (k c) -> p k c", k=nk)
                h = nk // 2
                load(layer_base(l) + i, s, [(dst[:, 0:h], rows(w, k0, h, c0, ncols)),
                                            (dst[:, h:nk], rows(w, k0 + h, h, c0, ncols))])

            def gate_up(part, wg, wu, pos, half, i, slot):
                dst = raw[:, slot, :].rearrange("p (k g c) -> p k g c", k=4, g=2)
                src = [w[half * 512:(half + 1) * 512, bass.ds(i * UF, UF)].rearrange("(k p) c -> p k c", p=P)
                       for w in (wg, wu)]
                load(part.base + pos, slot, [(dst[:, :, g, :], src[g]) for g in range(2)])

            def down(part, wd, pos, i, slot):
                dst = raw[:, slot, :].rearrange("p (k c) -> p k c", k=2)
                load(part.base + pos, slot, [(dst[:, k, :], wd[bass.ds(i * UF + k * P, P), :]) for k in range(2)])

            def ffn(part, wg, wu, wd):
                gate_up(part, wg, wu, 0, 0, 0, HEAD_SLOTS[0])
                gate_up(part, wg, wu, 1, 1, 0, HEAD_SLOTS[1])
                with sp.Fori(0, LOADS) as k:
                    for u in range(2):
                        i = 2 * k + 1 + u
                        pos = 2 + 6 * k + 3 * u
                        gate_up(part, wg, wu, pos, 0, i, 3 * u)
                        gate_up(part, wg, wu, pos + 1, 1, i, 3 * u + 1)
                        down(part, wd, pos + 2, i - 1, 3 * u + 2)
                down(part, wd, FFN_BLOCKS - 1, UNITS - 1, TAIL_SLOT)

            sp.dma_start(xs[:, :, :], x[0].rearrange("(t p) d -> p t d", p=P)).then_inc(x_landed, 16)
            sp.dma_start(cst[:, 0:C_NEG], consts[:, 0:C_NEG]).then_inc(ident_landed, 16)
            sp.dma_start(prm[:, 0, 0:Q_FFN_G], params[:, 0, 0:Q_FFN_G]).then_inc(gains_landed, 16)
            for i in range(MIX_BLOCKS):
                mixer_block(0, i)
                if i == 2:
                    sp.dma_start(prm[:, 0, Q_FFN_G:], params[:, 0, Q_FFN_G:]).then_inc(p_landed[0], 16)
                    sp.dma_start(cst[:, C_NEG:], consts[:, C_NEG:]).then_inc(c_landed, 16)
                if i == 8:
                    sp.dma_start(prm[:, 1, :], params[:, 1, :]).then_inc(p_landed[1], 16)
                    sp.dma_start(rw32[:, :], router).then_inc(p_landed[1], 16)
            ffn(Dense, dense_gate[0], dense_up[0], dense_down[0])
            for i in range(MIX_BLOCKS):
                mixer_block(1, i)
            with sp.Fori(0, E) as j:
                ffn(job_part(j), moe_gate[0, j], moe_up[0, j], moe_down[0, j])
            sp.wait_ge(route_ready, 1)
            sp.dma_start(row_g[:, :], final_g).then_inc(final_g_landed, 16)
            njobs = sp.value_load(jobs[0:1, 0:1], min_val=E, max_val=E + EXTRA)
            with sp.If(njobs > E):
                with sp.Fori(E, njobs) as j:
                    e = sp.value_load(jobs[0:1, bass.ds(j - (E - 1), 1)], min_val=0, max_val=E - 1)
                    ffn(job_part(j), moe_gate[0, e], moe_up[0, e], moe_down[0, e])
            for t in range(NT):
                sp.wait_ge(out_done, t + 1)
                sp.dma_start(out[0, t * P:(t + 1) * P, :], nat[:, t, :]).then_inc(out_landed, 16)
            sp.wait_ge(out_landed, 16 * NT)

        @block.gpsimd
        def _(pool):
            pool.memset(uT[:, :, :], 0.0).then_inc(padded, 1)
            pool.memset(zeros[:, :], 0.0).then_inc(padded, 1)
            pool.wait_ge(c_landed, 16)
            pool.tensor_copy(id_b[:, :], cst[:, C_ID:C_ID + P]).then_inc(biases_ready, 1)
            pool.tensor_copy(neg_b[:, :], cst[:, C_NEG:C_NEG + Z]).then_inc(biases_ready, 1)
            steps = 0
            for l in range(DEPTH):
                pool.wait_ge(conv_in, l + 1)
                if l == 1:
                    pool.wait_ge(p_landed[1], 32)
                for tap in range(DVE_TAPS, TAPS):
                    c = Q_CONV_W + tap
                    w = prm[:, l, c:c + (CH - 1) * TAPS + 1:TAPS].unsqueeze(2).to_broadcast([P, CH, T])
                    first = tap == DVE_TAPS
                    pool.tensor_tensor(cP[:, :, :] if first else tapped, uT[:, :, tap:tap + T], w, ALU.mult)\
                        .then_inc(pool_step, 1)
                    steps += 1
                    pool.wait_ge(pool_step, steps)
                    if not first:
                        pool.tensor_tensor(cP[:, :, :], cP[:, :, :], tapped, ALU.add).then_inc(pool_step, 1)
                        steps += 1
                        pool.wait_ge(pool_step, steps)
            pool.wait_ge(nat_ready, 10)
            pool.dma_start(row_g[:, :], moe_g).then_inc(moe_g_landed, 16)

        @block.scalar
        def _(act):
            def hi(n, slot, fill, b):
                act.wait_ge(slot_landed[slot], FILL * fill)
                if not (isinstance(n, int) and n < 3):
                    act.wait_ge(blocks_used, n - 2)
                act.activation(whi[:, b, :], raw[:, slot, :], ACT.Copy).then_inc(split_hi, 1)

            def mixer_hi(l, i):
                n = layer_base(l) + i
                hi(n, raw_slot(i), mixer_fill(l, i), n % 3)

            def rsqrt(m, cols, c0):
                act.wait_ge(var_ready, m + 1)
                act.activation(st[:, c0 + 16:c0 + 16 + cols], st[:, c0:c0 + cols], ACT.Ln).then_inc(ln_done, 1)
                act.wait_ge(ln_done, m + 1)
                act.activation(st[:, c0 + 32:c0 + 32 + cols], st[:, c0 + 16:c0 + 16 + cols], ACT.Exp, scale=-0.5)\
                    .then_inc(rsqrt_rough, 1)

            def sum_squares(src, width, c, n):
                if n > 1:
                    act.wait_ge(sumsq_done, n - 1)
                act.activation(junk[:, 0:width], src, ACT.Square, accum_out=st[:, c:c + 1]).then_inc(sumsq_done, 1)

            def turn_hi(e, gcol, l, bs=range(4)):
                for b in bs:
                    act.wait_ge(turned, 4 * e + b + 1)
                    if gcol is None:
                        act.activation(xT_hi[:, 2 * b:2 * b + 2, :], bank[turn_banks(e)[b]][:, :]
                                       .rearrange("p (k t) -> p k t", k=2), ACT.Copy).then_inc(xT_hi_ready, 2)
                        continue
                    for k in (2 * b, 2 * b + 1):
                        act.activation(xT_hi[:, k, :], bank[turn_banks(e)[b]][:, (k % 2) * T:(k % 2 + 1) * T], ACT.Copy,
                                       scale=prm[:, l, gcol + k:gcol + k + 1]).then_inc(xT_hi_ready, 1)

            def silu(part, i, u):
                act.wait_ge(blocks_used, part.base + gate_up_pos(i) + 1)
                for t in range(part.tiles):
                    act.activation(hs[:, t, :], bank[gu_bank(part, t, u)][:, 0:UF], ACT.Silu).then_inc(silu_ready, 1)

            def hT_hi_copy(part, i):
                w = part.tiles * P
                act.wait_ge(h_turned, part.unit0 + i + 1)
                act.activation(hT_hi[:, :, 0:w], bank[2][:, 0:2 * w].rearrange("p (f t) -> p f t", f=2), ACT.Copy)\
                    .then_inc(hT_hi_ready, 1)

            def unit(part, i, u, fill, between=None):
                pos = 3 * i - 1
                hi(part.base + pos, 3 * u, fill, buf(part, 2))
                if between:
                    between()
                hi(part.base + pos + 1, 3 * u + 1, fill, buf(part, 3))
                silu(part, i - 1, u)
                hi(part.base + pos + 2, 3 * u + 2, fill, buf(part, 4))
                hT_hi_copy(part, i - 1)

            def units(part, between=None):
                unit(part, 1, 0, part.loop_fills + 1, between)
                with act.Fori(0, PAIRS) as k:
                    for u in (1, 0):
                        unit(part, 2 * k + 3 - u, u, part.loop_fills + k + 2 - u)
                unit(part, UNITS - 1, 1, part.loop_fills + PAIRS + 1)
                hi(part.base + FFN_BLOCKS - 1, TAIL_SLOT, part.tail_fills + 1, buf(part, FFN_BLOCKS - 1))
                silu(part, UNITS - 1, 0)
                hT_hi_copy(part, UNITS - 1)

            def y_hi_copy(done):
                act.wait_ge(blocks_used, job_part(done).base)
                act.wait_ge(hotT_ready, done + 1)
                for n in range(2):
                    act.activation(y_hi[:, 4 * n:4 * n + 4, :], bank[3 + n][:, :].rearrange("p (k c) -> p k c", k=4),
                                   ACT.Copy, scale=slot_gate[:, 0:1]).then_inc(y_hi_ready, 1)

            def load_exp_and_ln():
                act.preload_act_table_set("natural_log_exp_and_others")

            norms = 0
            sums = 0
            for l in range(DEPTH):
                if l == 0:
                    load_exp_and_ln()
                    act.wait_ge(x_landed, 16)
                else:
                    mixer_hi(l, 0)
                    mixer_hi(l, 1)
                    load_exp_and_ln()
                for t in range(NT):
                    sums += 1
                    if l > 0:
                        act.wait_ge(x_updated, 8 * l - 2 + 2 * t)
                    sum_squares(xs[:, t, :], D, 48 + t, sums)
                rsqrt(norms, 2, 0)
                norms += 1
                if l == 0:
                    mixer_hi(l, 0)
                    act.wait_ge(gains_landed, 16)
                else:
                    act.wait_ge(p_landed[1], 32)
                turn_hi(3 * l, Q_ATTN_G, l)
                if l == 0:
                    mixer_hi(l, 1)
                mixer_hi(l, 2)
                mixer_hi(l, 3)
                act.wait_ge(blocks_used, layer_base(l) + 1)
                act.activation(sig[:, :, :], bank[0][:, :].rearrange("p (h t) -> p h t", h=CH), ACT.Sigmoid)\
                    .then_inc(gate_sig, 1)
                load_exp_and_ln()
                mixer_hi(l, 4)
                mixer_hi(l, 5)
                act.wait_ge(blocks_used, layer_base(l) + 3)
                act.activation(up_n[:, :, :], bank[1][:, :].rearrange("p (t c) -> p t c", t=NT), ACT.Copy)\
                    .then_inc(pool_in, 1)
                mixer_hi(l, 6)
                mixer_hi(l, 7)
                act.wait_ge(blocks_used, layer_base(l) + 5)
                for b in range(2):
                    act.activation(qT[:, 2 * b:2 * b + 2, :], bank[3 + b][:, :].rearrange("p (c t) -> p c t", c=2),
                                   ACT.Copy, scale=HD ** -0.5).then_inc(q_in, 1)
                mixer_hi(l, 8)
                mixer_hi(l, 9)
                if l == 0:
                    act.wait_ge(c_landed, 16)

                for s in range(HEADS + 2):
                    n = HEADS * l + s
                    cur = lnb[:, s % 2, :]
                    if s < HEADS:
                        act.wait_ge(z_ready, n + 1)
                        if n >= 2:
                            act.wait_ge(sp_ready, n - 1)
                        act.activation(cur, bank[1 + s % 3][:, 0:Z], ACT.Abs).then_inc(abs_done, 1)
                        act.wait_ge(abs_done, n + 1)
                        act.activation(cur, cur, ACT.Exp, scale=-1.0).then_inc(exp_done, 1)
                    if s >= 2:
                        act.wait_ge(c_ready, n - 1)
                        if n - 2 >= 2:
                            act.wait_ge(pv_done, n - 3)
                        act.activation(wgt[:, s % 2, :], bank[1 + (s - 2) % 3][:, 0:Z], ACT.Exp).then_inc(w_ready, 1)
                    if s < HEADS:
                        act.wait_ge(exp_done, n + 1)
                        act.activation(cur, cur, ACT.Ln, bias=cst[:, C_ONECOL:C_ONECOL + 1]).then_inc(ln_ready, 1)
                    if s == 1:
                        act.wait_ge(blocks_used, layer_base(l) + 9)
                        for t in range(NT):
                            act.activation(vn[:, t, :], bank[(0, 7)[t]][:, :], ACT.Copy).then_inc(v_in, 1)
                    if s == 2:
                        mixer_hi(l, 10)
                    if s == 4:
                        mixer_hi(l, 11)
                    if s == HEADS:
                        act.wait_ge(pool_out, l + 1)
                        for t in range(NT):
                            sums += 1
                            sum_squares(ob[:, t, :], POOL, 52 + t, sums)
                act.wait_ge(pv_done, HEADS * (l + 1))
                for t in range(NT):
                    sums += 1
                    sum_squares(bank[4 + t][:, :], ATTN, 50 + t, sums)
                act.wait_ge(conv_turned, l + 1)
                for t in range(NT):
                    sums += 1
                    sum_squares(bank[0][:, t * CONV:(t + 1) * CONV], CONV, 54 + t, sums)
                rsqrt(norms, 6, 0)
                norms += 1
                turn_hi(3 * l + 1, Q_GN_G, l, (0, 1))
                act.wait_ge(lin_ready, l + 1)
                act.activation(cn[:, :, :], cn[:, :, :], ACT.Silu).then_inc(swish_done, 1)
                act.wait_ge(swish_done, l + 1)
                for t in range(NT):
                    sums += 1
                    sum_squares(cn[:, t, :], CONV, 56 + t, sums)
                load_exp_and_ln()
                rsqrt(norms, 2, 6)
                norms += 1
                turn_hi(3 * l + 1, Q_GN_G, l, (2, 3))
                mixer_hi(l, 12)
                if l == 0:
                    hi(Dense.base, HEAD_SLOTS[0], Dense.head_fills + 1, buf(Dense, 0))
                    hi(Dense.base + 1, HEAD_SLOTS[1], Dense.tail_fills + 1, buf(Dense, 1))
                else:
                    act.activation(rw[:, :, 0, :], rw32[:, :].rearrange("p (k e) -> p k e", k=KD), ACT.Copy)\
                        .then_inc(rw_hi_ready, 1)
                for t in range(NT):
                    act.wait_ge(x_updated, 8 * l + 3 + t)
                    sums += 1
                    sum_squares(xs[:, t, :], D, 48 + t, sums)
                rsqrt(norms, 2, 0)
                norms += 1
                turn_hi(3 * l + 2, Q_FFN_G if l == 0 else None, l)
                if l == 1:
                    act.activation(xn_hi[:, :, :], nat[:, :, :], ACT.Copy).then_inc(xn_hi_ready, 1)
                if l == 0:
                    act.activation(st[:, 62:63], cst[:, C_ONECOL:C_ONECOL + 1], ACT.Silu).then_inc(table_ready, 1)
                    units(Dense)
            act.wait_ge(gap_ready, 1)
            act.activation(rt[:, R_EXP:R_EXP + NT], rt[:, R_GAP:R_GAP + NT], ACT.Exp).then_inc(gap_exp, 1)
            act.wait_ge(table_ready, 1)
            act.activation(st[:, 62:63], cst[:, C_ONECOL:C_ONECOL + 1], ACT.Silu).then_inc(table_ready, 1)
            act.wait_ge(njobs_ready, 1)
            njobs = act.value_load(jobs[0:1, 0:1], min_val=E, max_val=E + EXTRA)
            with act.Fori(0, njobs) as j:
                part = job_part(j)
                hi(part.base, HEAD_SLOTS[0], part.head_fills + 1, buf(part, 0))
                for b in range(2):
                    act.wait_ge(gathered, 2 * j + b + 1)
                    act.activation(xeT_hi[:, 4 * b:4 * b + 4, :], bank[5 + b][:, :].rearrange("p (k c) -> p k c", k=4),
                                   ACT.Copy).then_inc(xe_hi_ready, 1)
                hi(part.base + 1, HEAD_SLOTS[1], part.tail_fills + 1, buf(part, 1))
                units(part, lambda: y_hi_copy(j))
            load_exp_and_ln()
            y_hi_copy(njobs)
            act.wait_ge(added, 4 * njobs + 4)
            for t in range(NT):
                sums += 1
                sum_squares(xs[:, t, :], D, 48 + t, sums)
            rsqrt(norms, 2, 0)

        @block.vector
        def _(dve):
            steps = [0]

            def link(ins):
                steps[0] += 1
                ins.then_inc(dve_step, 1)
                dve.wait_ge(dve_step, steps[0])

            def lo(n, slot, b):
                dve.wait_ge(split_hi, n + 1)
                dve.tensor_tensor(wlo[:, b, :], raw[:, slot, :], whi[:, b, :].bitcast(F32), ALU.subtract)\
                    .then_inc(split_lo, 1)

            def mixer_lo(l, i):
                n = layer_base(l) + i
                lo(n, raw_slot(i), n % 3)

            def newton(m, cols, c0):
                v, y, u = (st[:, a:a + cols] for a in (c0, c0 + 32, c0 + 16))
                dve.wait_ge(rsqrt_rough, m + 1)
                link(dve.tensor_tensor(u, y, y, ALU.mult))
                link(dve.tensor_tensor(u, u, v, ALU.mult))
                link(dve.tensor_scalar(u, u, -0.5, 1.5, ALU.mult, ALU.add))
                link(dve.tensor_tensor(y, y, u, ALU.mult))

            def norm_rows(m, sums, gains=None):
                dve.wait_ge(sumsq_done, sums)
                dve.tensor_scalar(st[:, 0:2], st[:, 48:50], 1.0 / D, RMS_EPS, ALU.mult, ALU.add).then_inc(var_ready, 1)
                dve.wait_ge(var_ready, m + 1)
                newton(m, 2, 0)
                for t in range(NT):
                    if gains is None:
                        ins = dve.tensor_scalar(nat[:, t, :], xs[:, t, :], st[:, 32 + t:33 + t], None, ALU.mult)
                    else:
                        ins = dve.scalar_tensor_tensor(nat[:, t, :], xs[:, t, :], st[:, 32 + t:33 + t], gains,
                                                       ALU.mult, ALU.mult)
                    ins.then_inc(nat_ready, 1)

            def turn_lo(e, gcol, l, bs=range(4)):
                for b in bs:
                    dve.wait_ge(xT_hi_ready, 8 * e + 2 * b + 2)
                    if gcol is None:
                        dve.tensor_tensor(xT_lo[:, 2 * b:2 * b + 2, :], bank[turn_banks(e)[b]][:, :]
                                          .rearrange("p (k t) -> p k t", k=2), xT_hi[:, 2 * b:2 * b + 2, :].bitcast(F32),
                                          ALU.subtract).then_inc(xT_lo_ready, 2)
                        continue
                    for k in (2 * b, 2 * b + 1):
                        dve.scalar_tensor_tensor(xT_lo[:, k, :], bank[turn_banks(e)[b]][:, (k % 2) * T:(k % 2 + 1) * T],
                                                 prm[:, l, gcol + k:gcol + k + 1], xT_hi[:, k, :].bitcast(F32),
                                                 ALU.mult, ALU.subtract).then_inc(xT_lo_ready, 1)

            def gated(part, i, u):
                for t in range(part.tiles):
                    dve.wait_ge(silu_ready, part.gu0 + part.tiles * i + t + 1)
                    dve.tensor_tensor(hn[:, t, :], bank[gu_bank(part, t, u)][:, UF:2 * UF], hs[:, t, :], ALU.mult)\
                        .then_inc(h_ready, 1)

            def hT_lo_copy(part, i):
                w = part.tiles * P
                dve.wait_ge(hT_hi_ready, part.unit0 + i + 1)
                dve.tensor_tensor(hT_lo[:, :, 0:w], bank[2][:, 0:2 * w].rearrange("p (f t) -> p f t", f=2),
                                  hT_hi[:, :, 0:w].bitcast(F32), ALU.subtract).then_inc(hT_lo_ready, 1)

            def unit(part, i, u, between=None):
                pos = 3 * i - 1
                lo(part.base + pos, 3 * u, buf(part, 2))
                if between:
                    between()
                    gated(part, i - 1, u)
                    lo(part.base + pos + 1, 3 * u + 1, buf(part, 3))
                else:
                    lo(part.base + pos + 1, 3 * u + 1, buf(part, 3))
                    gated(part, i - 1, u)
                lo(part.base + pos + 2, 3 * u + 2, buf(part, 4))
                hT_lo_copy(part, i - 1)

            def units(part, between=None, after_unit1=None, before_last=None):
                unit(part, 1, 0, between)
                if after_unit1:
                    after_unit1()
                with dve.Fori(0, PAIRS) as k:
                    for u in (1, 0):
                        unit(part, 2 * k + 3 - u, u)
                if before_last:
                    before_last()
                unit(part, UNITS - 1, 1)
                lo(part.base + FFN_BLOCKS - 1, TAIL_SLOT, buf(part, FFN_BLOCKS - 1))
                gated(part, UNITS - 1, 0)
                hT_lo_copy(part, UNITS - 1)

            def add_to_x(t, n, b, s):
                dve.tensor_tensor(xs[:, t, n * 512:(n + 1) * 512], xs[:, t, n * 512:(n + 1) * 512], bank[b][:, :],
                                  ALU.add).then_inc(s, 1)

            def y_lo_copy(done):
                for n in range(2):
                    dve.wait_ge(y_hi_ready, 2 * done + n + 1)
                    dve.scalar_tensor_tensor(y_lo[:, 4 * n:4 * n + 4, :], bank[3 + n][:, :].rearrange("p (k c) -> p k c", k=4),
                                             slot_gate[:, 0:1], y_hi[:, 4 * n:4 * n + 4, :].bitcast(F32),
                                             ALU.mult, ALU.subtract).then_inc(y_lo_ready, 1)

            def add_scattered(done):
                for q in range(4):
                    dve.wait_ge(scattered, 4 * done + q + 1)
                    add_to_x(q // 2, q % 2, SCATTER_BANKS[q], added)

            def conv(l, steps):
                for s in steps:
                    tap, h = s // CH, s % CH
                    done = l * DVE_STEPS + s
                    w = prm[:, l, Q_CONV_W + h * TAPS + tap:Q_CONV_W + h * TAPS + tap + 1]
                    src = uT[:, h, tap:tap + T]
                    if tap == 0:
                        if h == 0:
                            dve.wait_ge(conv_in, l + 1)
                        dve.tensor_scalar(cT[:, h, :], src, w, prm[:, l, Q_CONV_B + h:Q_CONV_B + h + 1],
                                          ALU.mult, ALU.add).then_inc(conv_step, 1)
                    else:
                        dve.wait_ge(conv_step, done - CH + 1)
                        dve.scalar_tensor_tensor(cT[:, h, :], src, w, cT[:, h, :], ALU.mult, ALU.add)\
                            .then_inc(conv_step, 1)

            def job_rows(r, n):
                return rt[:, r * JOBCOLS:(r + n) * JOBCOLS].rearrange("p (r j) -> p r j", r=n)

            def one_hot(j):
                for t in range(NT):
                    dve.tensor_scalar(hot[:, t, :], cst[:, C_IOTA:C_IOTA + CAP],
                                      rt[:, bass.ds((J_RANK + t) * JOBCOLS + j, 1)],
                                      rt[:, bass.ds((J_MASK + t) * JOBCOLS + j, 1)],
                                      ALU.is_equal, ALU.mult).then_inc(hot_ready, 1)

            norms = 0
            sums = 0
            for l in range(DEPTH):
                sums += 2
                norm_rows(norms, sums)
                norms += 1
                if l == 0:
                    mixer_lo(l, 0)
                    dve.wait_ge(gains_landed, 16)
                turn_lo(3 * l, Q_ATTN_G, l)
                if l == 0:
                    mixer_lo(l, 1)
                mixer_lo(l, 2)
                mixer_lo(l, 3)
                mixer_lo(l, 4)
                mixer_lo(l, 5)
                dve.wait_ge(blocks_used, layer_base(l) + 3)
                dve.wait_ge(gate_sig, l + 1)
                if l == 0:
                    dve.wait_ge(padded, 2)
                    dve.wait_ge(p_landed[0], 16)
                dve.tensor_tensor(uT[:, :, TAPS - 1:], bank[2][:, :].rearrange("p (h t) -> p h t", h=CH), sig[:, :, :],
                                  ALU.mult).then_inc(conv_in, 1)
                mixer_lo(l, 6)
                conv(l, range(0, 10))
                mixer_lo(l, 7)
                conv(l, range(10, 20))
                dve.wait_ge(blocks_used, layer_base(l) + 7)
                for b in range(2):
                    dve.tensor_copy(kT[:, 2 * b:2 * b + 2, :], bank[5 + b][:, :].rearrange("p (c t) -> p c t", c=2))\
                        .then_inc(k_in, 1)
                mixer_lo(l, 8)
                conv(l, range(20, 22))
                mixer_lo(l, 9)
                conv(l, range(22, 26))
                done = 26
                for s in range(HEADS):
                    n = HEADS * l + s
                    dve.wait_ge(ln_ready, n + 1)
                    if n >= 2:
                        dve.wait_ge(c_ready, n - 1)
                    dve.scalar_tensor_tensor(sp_b[:, s % 2, :], bank[1 + s % 3][:, 0:Z], 0.0, lnb[:, s % 2, :],
                                             ALU.max, ALU.add).then_inc(sp_ready, 1)
                    if s in (2, 4):
                        mixer_lo(l, 10 + (s - 2) // 2)
                    if s == 3:
                        dve.wait_ge(pool_mixed, l + 1)
                        dve.tensor_copy(yT[:, :, :], bank[6][:, :].rearrange("p (g t) -> p g t", g=2)).then_inc(yT_ready, 1)
                    if s == 6:
                        dve.wait_ge(pool_done, l + 1)
                        for odd in range(2):
                            rows = ob[:, :, :].rearrange("p t (g o c) -> p t g o c", g=2, o=2)[:, :, :, odd, :]
                            scale = prm[:, l, Q_POOL_S:Q_POOL_S + POOL].rearrange("p (g o c) -> p g o c", g=2, o=2)
                            ins = dve.tensor_tensor(rows, bank[7 - odd][:, 0:NT * P].rearrange("p (t g c) -> p t g c", t=NT, g=2),
                                                    scale[:, :, odd, :].unsqueeze(1).to_broadcast([P, NT, 2, HD]), ALU.mult)
                        ins.then_inc(pool_out, 1)
                    more = min(DVE_STEPS, done + CONV_STEPS[s])
                    conv(l, range(done, more))
                    done = more
                dve.wait_ge(conv_step, DVE_STEPS * (l + 1))
                dve.wait_ge(pool_step, (2 * POOL_TAPS - 1) * (l + 1))
                dve.tensor_tensor(cT[:, :, :], cT[:, :, :], cP[:, :, :], ALU.add).then_inc(conv_joined, 1)
                sums += 6
                dve.wait_ge(sumsq_done, sums)
                dve.tensor_scalar(st[:, 4:6], st[:, 50:52], 1.0 / ATTN, RMS_EPS, ALU.mult, ALU.add)
                dve.tensor_scalar(st[:, 2:4], st[:, 52:54], 1.0 / POOL, RMS_EPS, ALU.mult, ALU.add)
                dve.tensor_scalar(st[:, 0:2], st[:, 54:56], 1.0 / CONV, LN_EPS, ALU.mult, ALU.add).then_inc(var_ready, 1)
                dve.wait_ge(var_ready, norms + 1)
                newton(norms, 6, 0)
                norms += 1
                for t in range(NT):
                    dve.tensor_scalar(nat[:, t, 0:ATTN], bank[4 + t][:, :], st[:, 36 + t:37 + t], None, ALU.mult)\
                        .then_inc(attn_nat_ready, 1)
                for t in range(NT):
                    ins = dve.scalar_tensor_tensor(cn[:, t, :], bank[0][:, t * CONV:(t + 1) * CONV], st[:, 32 + t:33 + t],
                                                   prm[:, l, Q_LN_G:Q_LN_G + CONV], ALU.mult, ALU.mult)
                link(ins)
                dve.tensor_tensor(cn[:, :, :], cn[:, :, :], prm[:, l, Q_LN_B:Q_LN_B + CONV].unsqueeze(1)
                                  .to_broadcast([P, NT, CONV]), ALU.add).then_inc(lin_ready, 1)
                turn_lo(3 * l + 1, Q_GN_G, l, (0, 1))
                for t in range(NT):
                    dve.tensor_scalar(nat[:, t, ATTN:ATTN + POOL], ob[:, t, :], st[:, 34 + t:35 + t], None, ALU.mult)
                sums += 2
                dve.wait_ge(sumsq_done, sums)
                dve.tensor_scalar(st[:, 6:8], st[:, 56:58], 1.0 / CONV, RMS_EPS, ALU.mult, ALU.add).then_inc(var_ready, 1)
                dve.wait_ge(var_ready, norms + 1)
                newton(norms, 2, 6)
                norms += 1
                for t in range(NT):
                    dve.tensor_scalar(nat[:, t, ATTN + POOL:D], cn[:, t, :], st[:, 38 + t:39 + t], None, ALU.mult)\
                        .then_inc(nat_ready, 1)
                turn_lo(3 * l + 1, Q_GN_G, l, (2, 3))
                mixer_lo(l, 12)
                if l == 0:
                    lo(Dense.base, HEAD_SLOTS[0], buf(Dense, 0))
                for n in range(2):
                    dve.wait_ge(blocks_used, layer_base(l) + W_IN_BLOCKS + 2 + n + 1)
                    for t in range(NT):
                        add_to_x(t, n, OUT_BANKS[n][t], x_updated)
                    if n == 0:
                        if l == 0:
                            lo(Dense.base + 1, HEAD_SLOTS[1], buf(Dense, 1))
                        else:
                            dve.wait_ge(rw_hi_ready, 1)
                            dve.tensor_tensor(rw[:, :, 1, :], rw32[:, :].rearrange("p (k e) -> p k e", k=KD),
                                              rw[:, :, 0, :].bitcast(F32), ALU.subtract).then_inc(rw_lo_ready, 1)
                            link(dve.memset(rt[:, 0:J_ROWS * JOBCOLS], 0.0))
                            link(dve.tensor_copy(job_rows(J_EXPERT, 1)[:, :, 0:E], cst[:, C_EIDX:C_EIDX + E].unsqueeze(1)))
                sums += 2
                if l == 1:
                    dve.wait_ge(moe_g_landed, 16)
                norm_rows(norms, sums, row_g[:, :] if l == 1 else None)
                norms += 1
                turn_lo(3 * l + 2, Q_FFN_G if l == 0 else None, l)
                if l == 0:
                    units(Dense)
                    mixer_lo(1, 0)
                    mixer_lo(1, 1)
                    dve.wait_ge(blocks_used, LAYER_BLOCKS)
                    for q in range(4):
                        add_to_x(q // 2, q % 2, Dense.acc[q], x_updated)

            dve.wait_ge(xn_hi_ready, 1)
            dve.tensor_tensor(xn_lo[:, :, :], nat[:, :, :], xn_hi[:, :, :].bitcast(F32), ALU.subtract).then_inc(xn_lo_ready, 1)
            dve.wait_ge(logitsT_ready, 1)
            dve.tensor_copy(logitsT, bank[0][0:2 * E, 0:T]).then_inc(logitsT_copied, 1)

            def tiles8(c):
                return rt[:, c:c + NT * E].rearrange("p (t e) -> p t e", t=NT)

            def per_tile(c):
                return rt[:, c:c + NT].unsqueeze(2).to_broadcast([P, NT, E])

            eq, sel1, sel2, lg2, top, top2, best, g1, g2, over, cum, count = (
                R_OTHER + c for c in (0, 16, 32, 48, 64, 66, 68, 70, 72, 74, 82, 90))
            S, pairs_at = R_OTHER + 96, R_OTHER + 128
            logits = bank[6][:, 0:NT * E].rearrange("p (t e) -> p t e", t=NT)
            rev = cst[:, C_REV:C_REV + E].unsqueeze(1).to_broadcast([P, NT, E])
            dve.wait_ge(logits_ready, 1)
            for src, m, sel in ((logits, top, sel1), (tiles8(lg2), top2, sel2)):
                if sel == sel2:
                    link(dve.scalar_tensor_tensor(tiles8(lg2), tiles8(sel1), LOWEST, logits, ALU.mult, ALU.add))
                link(dve.tensor_reduce(rt[:, m:m + NT], src, AX, ALU.max))
                link(dve.tensor_tensor(tiles8(eq), src, per_tile(m), ALU.is_equal))
                link(dve.tensor_tensor(tiles8(eq), tiles8(eq), rev, ALU.mult))
                link(dve.tensor_reduce(rt[:, best:best + NT], tiles8(eq), AX, ALU.max))
                link(dve.tensor_tensor(tiles8(sel), rev, per_tile(best), ALU.is_equal))
            masks, ranks, gates = (job_rows(r, NT)[:, :, 0:E] for r in (J_MASK, J_RANK, J_GATE))
            dve.tensor_tensor(masks, tiles8(sel1), tiles8(sel2), ALU.add).then_inc(mask_ready, 1)
            dve.tensor_tensor(rt[:, R_GAP:R_GAP + NT], rt[:, top2:top2 + NT], rt[:, top:top + NT], ALU.subtract)\
                .then_inc(gap_ready, 1)
            dve.wait_ge(rank_ready, 1)
            dve.wait_ge(mask_ready, 1)
            dve.tensor_scalar(rt[:, over:over + E], bank[5][:, NT * E:(NT + 1) * E], float(CAP), None, ALU.is_gt)
            link(dve.tensor_copy(ranks, bank[5][:, 0:NT * E].rearrange("p (t e) -> p t e", t=NT)))
            one_hot(0)
            link(dve.tensor_reduce(rt[:, count:count + 1], rt[:, over:over + E], AX, ALU.add))
            dve.tensor_scalar(jobs[:, 0:1], rt[:, count:count + 1], float(E), None, ALU.add).then_inc(njobs_ready, 1)
            e2 = R_EXP
            dve.wait_ge(gap_exp, 1)
            link(dve.tensor_scalar(rt[:, g2:g2 + NT], rt[:, e2:e2 + NT], 1.0, None, ALU.add))
            link(dve.reciprocal(rt[:, g1:g1 + NT], rt[:, g2:g2 + NT]))
            link(dve.tensor_tensor(rt[:, g2:g2 + NT], rt[:, e2:e2 + NT], rt[:, g1:g1 + NT], ALU.mult))
            dve.tensor_tensor(tiles8(eq), tiles8(sel2), per_tile(g2), ALU.mult)
            link(dve.tensor_tensor(tiles8(sel1), tiles8(sel1), per_tile(g1), ALU.mult))
            link(dve.tensor_tensor(gates, tiles8(sel1), tiles8(eq), ALU.add))
            pairs = rt[:, pairs_at:pairs_at + E * E].rearrange("p (a b) -> p a b", a=E)
            link(dve.tensor_tensor(pairs, cst[:, C_TRIE:C_TRIE + E * E].rearrange("p (a b) -> p a b", a=E),
                                   rt[:, over:over + E].unsqueeze(1).to_broadcast([P, E, E]), ALU.mult))
            link(dve.tensor_reduce(rt[:, cum:cum + E], pairs, AX, ALU.add))
            s3 = rt[:, S:S + EXTRA * E].rearrange("p (o e) -> p o e", o=EXTRA)
            link(dve.tensor_tensor(s3, cst[:, C_OIDX:C_OIDX + EXTRA * E].rearrange("p (o e) -> p o e", o=EXTRA),
                                   rt[:, cum:cum + E].unsqueeze(1).to_broadcast([P, EXTRA, E]), ALU.is_equal))
            link(dve.tensor_tensor(s3, s3, rt[:, over:over + E].unsqueeze(1).to_broadcast([P, EXTRA, E]), ALU.mult))
            picked = rt[:, pairs_at:pairs_at + J_ROWS * EXTRA * E].rearrange("p (r o e) -> p r o e", r=J_ROWS, o=EXTRA)
            all_rows = job_rows(0, J_ROWS)
            link(dve.tensor_tensor(picked, all_rows[:, :, 0:E].unsqueeze(2).to_broadcast([P, J_ROWS, EXTRA, E]),
                                   s3.unsqueeze(1).to_broadcast([P, J_ROWS, EXTRA, E]), ALU.mult))
            link(dve.tensor_reduce(all_rows[:, :, E:E + EXTRA], picked, AX, ALU.add))
            more_ranks = job_rows(J_RANK, NT)[:, :, E:E + EXTRA]
            link(dve.tensor_scalar(more_ranks, more_ranks, -float(CAP), None, ALU.add))
            dve.memset(slot_gate[:, :], 0.0)
            dve.tensor_scalar(hotT[:, :], cst[:, C_POOL:C_POOL + T], 0.0, None, ALU.mult).then_inc(hotT_ready, 1)
            x0 = J_EXPERT * JOBCOLS + E
            dve.tensor_copy(jobs[:, 1:1 + EXTRA], rt[:, x0:x0 + EXTRA]).then_inc(route_ready, 1)

            dve.wait_ge(njobs_ready, 1)
            njobs = dve.value_load(jobs[0:1, 0:1], min_val=E, max_val=E + EXTRA)
            with dve.Fori(0, njobs) as j:
                part = job_part(j)
                lo(part.base, HEAD_SLOTS[0], buf(part, 0))
                for b in range(2):
                    dve.wait_ge(xe_hi_ready, 2 * j + b + 1)
                    dve.tensor_tensor(xeT_lo[:, 4 * b:4 * b + 4, :], bank[5 + b][:, :].rearrange("p (k c) -> p k c", k=4),
                                      xeT_hi[:, 4 * b:4 * b + 4, :].bitcast(F32), ALU.subtract).then_inc(xe_lo_ready, 1)
                lo(part.base + 1, HEAD_SLOTS[1], buf(part, 1))

                def add_and_keep_hot():
                    add_scattered(j)
                    dve.wait_ge(hot_turned, j + 1)
                    dve.tensor_copy(hotT[:, :], bank[7][:, 0:T])
                    dve.tensor_copy(slot_gate[:, :], bank[7][:, T:T + 1]).then_inc(hotT_ready, 1)

                units(part, lambda: y_lo_copy(j), add_and_keep_hot, lambda: one_hot(j + 1))
            y_lo_copy(njobs)
            add_scattered(njobs)
            sums += 2
            dve.wait_ge(sumsq_done, sums)
            dve.tensor_scalar(st[:, 0:2], st[:, 48:50], 1.0 / D, RMS_EPS, ALU.mult, ALU.add).then_inc(var_ready, 1)
            dve.wait_ge(var_ready, norms + 1)
            newton(norms, 2, 0)
            dve.wait_ge(final_g_landed, 16)
            for t in range(NT):
                dve.scalar_tensor_tensor(nat[:, t, :], xs[:, t, :], st[:, 32 + t:33 + t], row_g[:, :], ALU.mult, ALU.mult)\
                    .then_inc(out_done, 1)

        @block.tensor
        def _(pe):
            def three(out_ap, l_hi, l_lo, r_hi, r_lo, start, stop, **kw):
                pe.matmul(out_ap, l_hi, r_hi, start=start, stop=False, **kw)
                pe.matmul(out_ap, l_hi, r_lo, start=False, stop=False, **kw)
                return pe.matmul(out_ap, l_lo, r_hi, start=False, stop=stop, **kw)

            def turn(e, bs=range(4)):
                if 3 not in bs:
                    pe.wait_ge(attn_nat_ready, 2 * (e // 3) + 2)
                else:
                    pe.wait_ge(nat_ready, 2 * e + 2)
                for b in bs:
                    for k in (2 * b, 2 * b + 1):
                        for t in range(NT):
                            c = (k % 2) * T + t * P
                            ins = pe.transpose(bank[turn_banks(e)[b]][:, c:c + P], nat[:, t, k * P:(k + 1) * P], ident)
                    ins.then_inc(turned, 1)

            def mixer_block(l, i):
                n = layer_base(l) + i
                pe.wait_ge(split_lo, n + 1)
                return whi[:, n % 3, :], wlo[:, n % 3, :]

            def turned_rows(e, kk):
                pe.wait_ge(xT_lo_ready, 8 * e + kk + 1)

            def rows_out(l, i, half, banks, fresh=None):
                wh, wl = mixer_block(l, i)
                for t in range(NT):
                    for k in range(4):
                        kk = 4 * half + k
                        if fresh is not None and t == 0:
                            turned_rows(fresh, kk)
                        ins = three(bank[banks[t]][:, :], xT_hi[:, kk, t * P:(t + 1) * P], xT_lo[:, kk, t * P:(t + 1) * P],
                                    wh[:, k * 512:(k + 1) * 512], wl[:, k * 512:(k + 1) * 512], kk == 0, kk == KD - 1)
                ins.then_inc(blocks_used, 1)

            def cols_out(l, i, k0, nk, width, first, outs, fresh=None):
                wh, wl = mixer_block(l, i)
                for c, o in enumerate(outs):
                    for k in range(nk):
                        a = k * width + first + c * P
                        kk = k0 + k
                        if fresh is not None and c == 0:
                            turned_rows(fresh, kk)
                        ins = three(o, wh[:, a:a + P], wl[:, a:a + P], xT_hi[:, kk, :], xT_lo[:, kk, :],
                                    kk == 0 and c % 2 == 0, kk == KD - 1, skip_group_check=True)
                return ins

            def halves(b):
                return [bank[b][:, 0:T], bank[b][:, T:2 * T]]

            def gate_up(part, pos, b, half, banks, fresh=None):
                pe.wait_ge(split_lo, part.base + pos + 1)
                for t in range(part.tiles):
                    for k in range(4):
                        kk = 4 * half + k
                        if fresh is not None and t == 0:
                            turned_rows(fresh, kk)
                        ins = three(bank[banks[t]][:, :], xT_hi[:, kk, t * P:(t + 1) * P], xT_lo[:, kk, t * P:(t + 1) * P],
                                    whi[:, b, k * 512:(k + 1) * 512], wlo[:, b, k * 512:(k + 1) * 512],
                                    kk == 0, kk == KD - 1)
                ins.then_inc(blocks_used, 1)

            def turn_h(part, i):
                w = part.tiles * P
                pe.wait_ge(h_ready, part.gu0 + part.tiles * (i + 1))
                for f in range(2):
                    for t in range(part.tiles):
                        ins = pe.transpose(bank[2][:, f * w + t * P:f * w + (t + 1) * P], hn[:, t, f * P:(f + 1) * P], ident)
                ins.then_inc(h_turned, 1)

            def down(part, pos, b, i, last):
                pe.wait_ge(split_lo, part.base + pos + 1)
                pe.wait_ge(hT_lo_ready, part.unit0 + i + 1)
                for t in range(part.tiles):
                    for f in range(2):
                        for n in range(2):
                            c = f * D + n * 512
                            ins = three(bank[part.acc[2 * t + n]][:, :], hT_hi[:, f, t * P:(t + 1) * P],
                                        hT_lo[:, f, t * P:(t + 1) * P], whi[:, b, c:c + 512], wlo[:, b, c:c + 512],
                                        False, last and f == 1, skip_group_check=True)
                ins.then_inc(blocks_used, 1)

            def prime(part):
                for b in part.acc:
                    pe.matmul(bank[b][:, :].rearrange("p (a c) -> p a c", a=4), zeros[:, :], zeros[:, :].unsqueeze(1).to_broadcast([P, 4, P]), start=True, stop=False, skip_group_check=True)

            def unit(part, i, u, after_a=None, after_b=None):
                pos = 3 * i - 1
                if part.tiles == NT:
                    pe.wait_ge(h_ready, part.gu0 + part.tiles * i)
                elif not after_a:
                    pe.wait_ge(added, 4 * part.parts)
                gate_up(part, pos, buf(part, 2), 0, gu_banks(part, 1 - u))
                if after_a:
                    after_a()
                turn_h(part, i - 1)
                gate_up(part, pos + 1, buf(part, 3), 1, gu_banks(part, 1 - u))
                if after_b:
                    after_b()
                down(part, pos + 2, buf(part, 4), i - 1, False)

            def ffn(part, after_a1=None, after_b1=None, tail_extra=None, fresh=None):
                gate_up(part, 0, buf(part, 0), 0, gu_banks(part, 0), fresh)
                gate_up(part, 1, buf(part, 1), 1, gu_banks(part, 0), fresh)
                if not after_a1:
                    prime(part)
                unit(part, 1, 0, after_a1, after_b1)
                with pe.Fori(0, PAIRS) as k:
                    for u in (1, 0):
                        unit(part, 2 * k + 3 - u, u)
                unit(part, UNITS - 1, 1)
                turn_h(part, UNITS - 1)
                if tail_extra:
                    tail_extra()
                down(part, FFN_BLOCKS - 1, buf(part, FFN_BLOCKS - 1), UNITS - 1, True)

            for l in range(DEPTH):
                if l == 0:
                    pe.wait_ge(ident_landed, 16)
                    pe.wait_ge(padded, 2)
                turn(3 * l)
                cols_out(l, 0, 0, KD, CONV, 0, halves(0), 3 * l).then_inc(blocks_used, 1)
                for half in range(2):
                    wh, wl = mixer_block(l, 1 + half)
                    for t in range(NT):
                        for k in range(4):
                            kk = 4 * half + k
                            three(halves(1)[t], xT_hi[:, kk, t * P:(t + 1) * P], xT_lo[:, kk, t * P:(t + 1) * P],
                                  wh[:, k * 512:k * 512 + POOL], wl[:, k * 512:k * 512 + POOL],
                                  kk == 0 and t == 0, kk == KD - 1, skip_group_check=True)
                    cols_out(l, 1 + half, 4 * half, 4, 512, POOL, halves(2)).then_inc(blocks_used, 1)
                for q, banks in ((0, (3, 4)), (1, (5, 6))):
                    for half in range(2):
                        cols_out(l, 3 + 2 * q + half, 4 * half, 4, 512, 0, halves(banks[0]) + halves(banks[1]))\
                            .then_inc(blocks_used, 1)
                pe.wait_ge(gate_sig, l + 1)
                pe.wait_ge(q_in, 2 * l + 2)
                pe.wait_ge(k_in, 2 * l + 2)
                pe.wait_ge(conv_in, l + 1)
                pe.wait_ge(pool_in, l + 1)
                if l == 0:
                    pe.wait_ge(biases_ready, 2)
                for s in range(HEADS + 3):
                    if s < HEADS:
                        n = HEADS * l + s
                        zb = bank[1 + s % 3]
                        if s >= 3:
                            pe.wait_ge(w_ready, n - 2)
                        r = slice((s % 2) * HD, (s % 2 + 1) * HD)
                        pe.matmul(zb[:, 0:Z], id_b[:, :], neg_b[:, :], start=True, stop=False, skip_group_check=True)
                        pe.matmul(zb[:, 0:T], kT[r, s // 2, 0:P], qT[r, s // 2, :], start=False, stop=False,
                                  skip_group_check=True)
                        pe.matmul(zb[:, T:Z], kT[r, s // 2, P:T], qT[r, s // 2, P:T], start=False, stop=True,
                                  skip_group_check=True).then_inc(z_ready, 1)
                    if s < 2:
                        rows_out(l, 7 + s, s, (0, 7))
                    if s >= 2 and s < HEADS + 2:
                        n = HEADS * l + s - 2
                        zb, sp_h = bank[1 + (s - 2) % 3], sp_b[:, s % 2, :]
                        pe.wait_ge(sp_ready, n + 1)
                        pe.matmul(zb[:, 0:T], cst[:, C_TRIN:C_TRIN + P], sp_h[:, 0:T], start=False, stop=False,
                                  skip_group_check=True)
                        pe.matmul(zb[:, P:T], cst[:, C_ONEN:C_ONEN + P], sp_h[:, T:Z], start=False, stop=False,
                                  skip_group_check=True)
                        pe.matmul(zb[:, T:Z], cst[:, C_TRIN:C_TRIN + P], sp_h[:, T:Z], start=False, stop=True,
                                  skip_group_check=True).then_inc(c_ready, 1)
                    if s == 2:
                        for g in range(len(WINDOWS)):
                            o = bank[6][(g % 2) * HD:(g % 2 + 1) * HD, (g // 2) * T:(g // 2 + 1) * T]
                            b0 = C_POOL + g * Z
                            pe.matmul(o, up_n[:, 0, g * HD:(g + 1) * HD], cst[:, b0:b0 + T], start=True, stop=False,
                                      skip_group_check=True)
                            ins = pe.matmul(o[:, P:T], up_n[:, 1, g * HD:(g + 1) * HD], cst[:, b0 + T:b0 + Z], start=False,
                                            stop=True, skip_group_check=True)
                        ins.then_inc(pool_mixed, 1)
                    if s >= 3:
                        n, h = HEADS * l + s - 3, s - 3
                        w = wgt[:, h % 2, :]
                        v0, v1 = (vn[:, t, h * HD:(h + 1) * HD] for t in range(NT))
                        if h == 0:
                            pe.wait_ge(v_in, 2 * l + 2)
                        pe.wait_ge(w_ready, n + 1)
                        pe.matmul(bank[4][:, h * HD:(h + 1) * HD], w[:, 0:P], v0, start=True, stop=True)
                        pe.matmul(bank[5][:, h * HD:(h + 1) * HD], w[:, P:T], v0, start=True, stop=False)
                        pe.matmul(bank[5][:, h * HD:(h + 1) * HD], w[:, T:Z], v1, start=False, stop=True).then_inc(pv_done, 1)
                    if s == 5:
                        pe.wait_ge(yT_ready, l + 1)
                        for t in range(NT):
                            for g in range(len(WINDOWS)):
                                r = slice((g % 2) * HD, (g % 2 + 1) * HD)
                                c = Q_POOL_W + (g // 2) * HD
                                o = t * P + (g // 2) * HD
                                ins = pe.matmul(bank[7 - g % 2][:, o:o + HD],
                                                yT[r, g // 2, t * P:(t + 1) * P], prm[r, l, c:c + HD], start=True, stop=True)
                        ins.then_inc(pool_done, 1)
                pe.wait_ge(conv_joined, l + 1)
                for t in range(NT):
                    for h in range(CH):
                        c = C_CENTRE + (1 - h) * P
                        ins = pe.matmul(bank[0][:, t * CONV:(t + 1) * CONV], cT[:, h, t * P:(t + 1) * P], cst[:, c:c + CONV],
                                        start=h == 0, stop=h == CH - 1)
                ins.then_inc(conv_turned, 1)
                for half in range(2):
                    turn(3 * l + 1, (2 * half, 2 * half + 1))
                    for n in range(2):
                        rows_out(l, W_IN_BLOCKS + 2 * half + n, half, OUT_BANKS[n], 3 * l + 1 if n == 0 else None)
                turn(3 * l + 2)
                if l == 0:
                    ffn(Dense, fresh=3 * l + 2)

            pe.wait_ge(rw_lo_ready, 1)
            for k in range(KD):
                w = rw[:, k, :, :].rearrange("p a e -> p (a e)")
                turned_rows(3 * (DEPTH - 1) + 2, k)
                pe.matmul(bank[0][0:2 * E, 0:T], w, xT_hi[:, k, :], start=k == 0, stop=False)
                ins = pe.matmul(bank[0][0:2 * E, 0:T], w, xT_lo[:, k, :], start=False, stop=k == KD - 1)
            ins.then_inc(logitsT_ready, 1)
            pe.wait_ge(logitsT_copied, 1)
            for t in range(NT):
                ins = pe.matmul(bank[6][:, t * E:(t + 1) * E], logitsT[:, t * P:(t + 1) * P], cst[0:2 * E, C_FOLD:C_FOLD + E],
                                start=True, stop=True)
            ins.then_inc(logits_ready, 1)
            pe.wait_ge(mask_ready, 1)
            m = [rt[:, (J_MASK + t) * JOBCOLS:(J_MASK + t) * JOBCOLS + E] for t in range(NT)]
            before, ones = cst[:, C_RANK:C_RANK + P], cst[:, C_ONE:C_ONE + P]
            o = [bank[5][:, c * E:(c + 1) * E] for c in range(3)]
            pe.matmul(o[0], before, m[0], start=True, stop=True)
            pe.matmul(o[1], ones, m[0], start=True, stop=False)
            pe.matmul(o[1], before, m[1], start=False, stop=True)
            pe.matmul(o[2], ones, m[0], start=True, stop=False)
            pe.matmul(o[2], ones, m[1], start=False, stop=True).then_inc(rank_ready, 1)

            def gather(j):
                pe.wait_ge(hot_ready, 2 * j + 2)
                for b in range(2):
                    for k in range(4 * b, 4 * b + 4):
                        o = bank[5 + b][:, (k % 4) * CAP:(k % 4 + 1) * CAP]
                        for t in range(NT):
                            pe.matmul(o, xn_hi[:, t, k * P:(k + 1) * P], hot[:, t, :], start=t == 0, stop=False)
                            ins = pe.matmul(o, xn_lo[:, t, k * P:(k + 1) * P], hot[:, t, :], start=False, stop=t == NT - 1)
                    ins.then_inc(gathered, 1)

            def scatter(done, with_unit0=True):
                pe.wait_ge(y_lo_ready, 2 * done + 2)
                for q in range(4):
                    t, n = q // 2, q % 2
                    if q == 3 and with_unit0:
                        pe.wait_ge(h_ready, job_part(done).gu0 + 1)
                    o = bank[SCATTER_BANKS[q]][:, :].rearrange("p (k c) -> p k c", k=4)
                    pe.matmul(o, hotT[:, t * P:(t + 1) * P], y_hi[:, 4 * n:4 * n + 4, :], start=True, stop=False)
                    pe.matmul(o, hotT[:, t * P:(t + 1) * P], y_lo[:, 4 * n:4 * n + 4, :], start=False, stop=True)\
                        .then_inc(scattered, 1)

            pe.wait_ge(xn_lo_ready, 1)
            gather(0)
            pe.wait_ge(njobs_ready, 1)
            njobs = pe.value_load(jobs[0:1, 0:1], min_val=E, max_val=E + EXTRA)
            with pe.Fori(0, njobs) as j:
                part = job_part(j)

                def scatter_and_prime():
                    scatter(j)
                    prime(part)

                def turn_hot():
                    pe.wait_ge(added, 4 * j + 1)
                    for t in range(NT):
                        pe.transpose(bank[7][:, t * P:(t + 1) * P], hot[:, t, :].bitcast(F32), ident)
                    for t in range(NT):
                        ins = pe.matmul(bank[7][:, T:T + 1], hot[:, t, :].bitcast(F32),
                                        rt[:, bass.ds((J_GATE + t) * JOBCOLS + j, 1)], start=t == 0, stop=t == NT - 1,
                                        skip_group_check=True)
                    ins.then_inc(hot_turned, 1)

                pe.wait_ge(xe_lo_ready, 2 * j + 2)
                ffn(part, scatter_and_prime, turn_hot, lambda: gather(j + 1))
            scatter(njobs, False)


SCATTER_BANKS = (7, 5, 6, 0)
OUT_BANKS = ((6, 7), (4, 5))
CONV_STEPS = (2, 2, 0, 2, 0, 2, 0, 0)


def gate_up_pos(i):
    return 3 * i + (i < 1)


def turn_banks(e):
    return (1, 2, 3, 1) if e % 3 == 1 else (4, 5, 6, 7)


def gu_bank(part, t, u):
    return t if part.tiles == NT else u


def gu_banks(part, u):
    return [gu_bank(part, t, u) for t in range(part.tiles)]


def _columns(v):
    return v.reshape(-1, P).T


def _params(inp):
    rows = []
    for l in range(DEPTH):
        cw = inp["conv_w"][l].reshape(TAPS, CH, P).transpose(2, 1, 0).reshape(P, CH * TAPS)
        pw = inp["pool_w"][l].reshape(2, 2, HD, HD).transpose(1, 2, 0, 3).reshape(P, 2 * HD)
        wide = [np.broadcast_to(inp[k][l][None, :], (P, inp[k].shape[1])) for k in ("pool_scale", "conv_ln_g", "conv_ln_b")]
        rows.append(np.concatenate([_columns(inp["attn_norm_g"][l]), _columns(inp["ffn_norm_g"][l]),
                                    _columns(inp["group_norm_g"][l]), cw, _columns(inp["conv_b"][l]), pw, *wide], axis=1))
    return np.ascontiguousarray(np.stack(rows, axis=1))


def kernel(**inputs):
    import concourse.bacc as bacc
    from concourse.bass_utils import run_bass_kernel_spmd

    inp = {k: np.asarray(v) for k, v in inputs.items()}
    arrays = {
        "x": inp["x"], "w_in": inp["w_in"], "w_out": inp["w_out"],
        "dense_gate": inp["dense_w_gate"], "dense_up": inp["dense_w_up"], "dense_down": inp["dense_w_down"],
        "moe_gate": inp["moe_w_gate"], "moe_up": inp["moe_w_up"], "moe_down": inp["moe_w_down"],
        "params": _params(inp),
        "router": np.ascontiguousarray(inp["router_w"][0].reshape(KD, P, E).transpose(1, 0, 2).reshape(P, KD * E)),
        "moe_g": np.ascontiguousarray(np.broadcast_to(inp["ffn_norm_g"][1][None, :], (P, D))),
        "final_g": np.ascontiguousarray(np.broadcast_to(inp["final_norm_g"][None, :], (P, D))),
        "consts": constants(),
    }
    arrays = {f"in_{k}": np.ascontiguousarray(a) for k, a in arrays.items()}
    nc = bacc.Bacc("TRN2", target_bir_lowering=False, num_devices=1)
    args = [nc.dram_tensor(k, a.shape, mybir.dt.from_np(a.dtype), kind="ExternalInput").ap() for k, a in arrays.items()]
    out = nc.dram_tensor("out", inp["x"].shape, F32, kind="ExternalOutput").ap()
    build(nc, *args, out)
    r = run_bass_kernel_spmd(nc, [arrays], core_ids=[0])
    return r.results[0]["out"]
```
